# Optimizing a Trainium2 kernel written in Bass

```python
import jax, jax.numpy as jnp
from jax import lax
import numpy as np

D_MODEL = 1024
BATCH = 1
SEQ = 256
DEPTH = 2
DEC_BATCH = 8
DEC_SEQ = 1
PAST_LEN = 2048
PAGE_SIZE = 128

MIX_WIDTH = D_MODEL
HG_WIDTH = MIX_WIDTH // 2
HG_HEADS = 4
HG_DK = HG_WIDTH // HG_HEADS
HG_DV = HG_WIDTH // HG_HEADS
HG_CHUNK = 64
LRU_WIDTH = MIX_WIDTH - HG_WIDTH
LRU_BLOCKS = 8
LRU_BW = LRU_WIDTH // LRU_BLOCKS
LRU_C = 8.0
CONV_K = 4
IN_WIDTH = 4 * HG_WIDTH + 2 * LRU_WIDTH
D_FF = 2816
N_EXPERTS = 8
TOP_K = 2
D_FF_EXPERT = 3584
N_DENSE = (DEPTH + 1) // 2
N_MOE = DEPTH // 2
EPS = 1e-6

kernel_name = 'hymba_style_hgrn2_rglru_decoder_step'

def rmsnorm(x, g):
    xf = x.astype(jnp.float32)
    y = xf * lax.rsqrt(jnp.mean(xf * xf, axis=-1, keepdims=True) + EPS)
    return (y * g.astype(jnp.float32)).astype(x.dtype)

def hgrn2_chunked(q, k, v, log_f, s0):
    B, L = q.shape[0], q.shape[1]
    C = min(HG_CHUNK, L)
    n_chunks = -(-L // C)
    pad = n_chunks * C - L
    if pad:
        pw = ((0, 0), (0, pad), (0, 0), (0, 0))
        q, k, v, log_f = [jnp.pad(t, pw) for t in (q, k, v, log_f)]

    def to_chunks(t):
        return t.reshape(B, n_chunks, C, t.shape[2], t.shape[3]).transpose(1, 0, 2, 3, 4)

    mask = jnp.tril(jnp.ones((C, C), dtype=bool))[None, :, :, None, None]

    def step(S, inp):
        qc, kc, vc, gc = inp
        b = jnp.cumsum(gc, axis=1)
        diff = b[:, :, None] - b[:, None, :]
        decay = jnp.exp(jnp.where(mask, diff, -jnp.inf))
        scores = jnp.sum(qc[:, :, None] * kc[:, None] * decay, axis=-1)
        o_intra = jnp.einsum('btsh,bshv->bthv', scores, vc)
        o_inter = jnp.einsum('bthk,bhkv->bthv', qc * jnp.exp(b), S)
        b_last = b[:, -1]
        k_dec = kc * jnp.exp(b_last[:, None] - b)
        S_new = jnp.exp(b_last)[..., None] * S + jnp.einsum('bshk,bshv->bhkv', k_dec, vc)
        return S_new, o_intra + o_inter

    S_fin, o = lax.scan(step, s0, (to_chunks(q), to_chunks(k), to_chunks(v), to_chunks(log_f)))
    o = o.transpose(1, 0, 2, 3, 4).reshape(B, n_chunks * C, HG_HEADS, HG_DV)[:, :L]
    return o, S_fin

def causal_conv(x, buf, w, b):
    L = x.shape[1]
    xx = jnp.concatenate([buf.astype(x.dtype), x], axis=1)
    y = b.astype(jnp.float32)
    for j in range(CONV_K):
        y = y + xx[:, j:j + L].astype(jnp.float32) * w[j].astype(jnp.float32)
    return y, xx[:, L:]

def lru_combine(e1, e2):
    a1, u1 = e1
    a2, u2 = e2
    return a1 * a2, a2 * u1 + u2

def mixer(h, s_hg, s_lru, s_conv, lb, w_in, hg_norm_g, conv_w, conv_b,
          w_ra, b_ra, w_ix, b_ix, lru_lambda, w_out):
    f32 = jnp.float32
    B, L, _ = h.shape
    z = h @ w_in
    splits = [HG_WIDTH, 2 * HG_WIDTH, 3 * HG_WIDTH, 4 * HG_WIDTH, 4 * HG_WIDTH + LRU_WIDTH]
    q_pre, f_pre, i_pre, g_pre, xr, gr = jnp.split(z, splits, axis=-1)

    shp = (B, L, HG_HEADS, HG_DK)
    q = jax.nn.silu(q_pre.astype(f32)).reshape(shp)
    fz = f_pre.astype(f32).reshape(shp)
    lbh = lb.reshape(HG_HEADS, HG_DK)
    log_f = jnp.logaddexp(jnp.log(lbh), jnp.log1p(-lbh) + jax.nn.log_sigmoid(fz))
    k = (1.0 - lbh) * jax.nn.sigmoid(-fz)
    v = i_pre.astype(f32).reshape(B, L, HG_HEADS, HG_DV)
    o, s_hg_new = hgrn2_chunked(q, k, v, log_f, s_hg.astype(f32))
    o = o * lax.rsqrt(jnp.mean(o * o, axis=-1, keepdims=True) + EPS)
    o = o * hg_norm_g.astype(f32).reshape(HG_HEADS, HG_DV)
    o = o.reshape(B, L, HG_WIDTH) * jax.nn.silu(g_pre.astype(f32))

    xc, conv_new = causal_conv(xr, s_conv, conv_w, conv_b)
    xcb = xc.reshape(B, L, LRU_BLOCKS, LRU_BW)
    r = jax.nn.sigmoid(jnp.einsum('blnc,ncd->blnd', xcb, w_ra.astype(f32))
                       + b_ra.astype(f32).reshape(LRU_BLOCKS, LRU_BW)).reshape(B, L, LRU_WIDTH)
    ig = jax.nn.sigmoid(jnp.einsum('blnc,ncd->blnd', xcb, w_ix.astype(f32))
                        + b_ix.astype(f32).reshape(LRU_BLOCKS, LRU_BW)).reshape(B, L, LRU_WIDTH)
    log_a = -LRU_C * jax.nn.softplus(-lru_lambda.astype(f32)) * r
    a = jnp.exp(log_a)
    u = jnp.sqrt(-jnp.expm1(2.0 * log_a)) * (ig * xc)
    u = u.at[:, 0].add(a[:, 0] * s_lru.astype(f32))
    _, hs = lax.associative_scan(lru_combine, (a, u), axis=1)
    lru_out = hs * jax.nn.gelu(gr.astype(f32))

    merged = jnp.concatenate([o, lru_out], axis=-1).astype(h.dtype)
    out = merged @ w_out
    return (out.astype(h.dtype), s_hg_new.astype(s_hg.dtype),
            hs[:, -1].astype(s_lru.dtype), conv_new.astype(s_conv.dtype))

def swiglu(h, w1, w3, w2):
    return (jax.nn.silu(h @ w1) * (h @ w3)) @ w2

def moe_ffn(h, router_w, w1, w3, w2):
    f32 = jnp.float32
    B, L, D = h.shape
    t = h.reshape(B * L, D)
    logits = (t @ router_w).astype(f32)
    top_v, top_i = lax.top_k(logits, TOP_K)
    probs = jax.nn.softmax(top_v, axis=-1)
    gates = jnp.sum(jax.nn.one_hot(top_i, N_EXPERTS, dtype=f32) * probs[..., None], axis=1)
    out = jnp.zeros((B * L, D), f32)
    for e in range(N_EXPERTS):
        y = swiglu(t, w1[e], w3[e], w2[e]).astype(f32)
        out = out + gates[:, e:e + 1] * y
    return out.astype(h.dtype).reshape(B, L, D)

def trunk(x, s_hg, s_lru, s_conv, norm1_g, w_in, lower_bounds, hg_norm_g, conv_w, conv_b,
          w_ra, b_ra, w_ix, b_ix, lru_lambda, w_out, norm2_g, ffn_w1, ffn_w3, ffn_w2,
          router_w, moe_w1, moe_w3, moe_w2, final_norm_g):
    lb_all = jnp.cumsum(jax.nn.softmax(lower_bounds.astype(jnp.float32), axis=0), axis=0)
    lb_all = lb_all - lb_all[0]
    new_hg, new_lru, new_conv = [], [], []
    for l in range(DEPTH):
        h = rmsnorm(x, norm1_g[l])
        m, s1, s2, s3 = mixer(h, s_hg[l], s_lru[l], s_conv[l], lb_all[l], w_in[l], hg_norm_g[l],
                              conv_w[l], conv_b[l], w_ra[l], b_ra[l], w_ix[l], b_ix[l],
                              lru_lambda[l], w_out[l])
        x = x + m
        new_hg.append(s1)
        new_lru.append(s2)
        new_conv.append(s3)
        h = rmsnorm(x, norm2_g[l])
        if l % 2 == 0:
            j = l // 2
            x = x + swiglu(h, ffn_w1[j], ffn_w3[j], ffn_w2[j]).astype(x.dtype)
        else:
            j = l // 2
            x = x + moe_ffn(h, router_w[j], moe_w1[j], moe_w3[j], moe_w2[j])
    y = rmsnorm(x, final_norm_g)
    return y, jnp.stack(new_hg), jnp.stack(new_lru), jnp.stack(new_conv)

def setup_inputs(seed: int = 0) -> dict:
    key = jax.random.key(seed)
    ks = jax.random.split(key, 32)
    f32 = jnp.float32

    def nrm(k, shape, scale):
        return jax.random.normal(k, shape, f32) * scale

    u = jax.random.uniform(ks[15], (DEPTH, LRU_WIDTH), f32, 0.9, 0.999)
    a0 = u ** (1.0 / LRU_C)
    return {
        'x_prompt': nrm(ks[0], (BATCH, SEQ, D_MODEL), 1.0),
        'x_sample': nrm(ks[1], (DEC_BATCH, DEC_SEQ, D_MODEL), 1.0),
        'state_hgrn': nrm(ks[2], (DEPTH, DEC_BATCH, HG_HEADS, HG_DK, HG_DV), 0.3),
        'state_lru': nrm(ks[3], (DEPTH, DEC_BATCH, LRU_WIDTH), 0.5),
        'state_conv': nrm(ks[4], (DEPTH, DEC_BATCH, CONV_K - 1, LRU_WIDTH), 1.0),
        'norm1_g': 1.0 + nrm(ks[5], (DEPTH, D_MODEL), 0.02),
        'w_in': nrm(ks[6], (DEPTH, D_MODEL, IN_WIDTH), D_MODEL ** -0.5),
        'lower_bounds': nrm(ks[7], (DEPTH, HG_WIDTH), 1.0),
        'hg_norm_g': 1.0 + nrm(ks[8], (DEPTH, HG_WIDTH), 0.02),
        'conv_w': nrm(ks[9], (DEPTH, CONV_K, LRU_WIDTH), CONV_K ** -0.5),
        'conv_b': nrm(ks[10], (DEPTH, LRU_WIDTH), 0.01),
        'w_ra': nrm(ks[11], (DEPTH, LRU_BLOCKS, LRU_BW, LRU_BW), LRU_BW ** -0.5),
        'b_ra': nrm(ks[12], (DEPTH, LRU_WIDTH), 0.01),
        'w_ix': nrm(ks[13], (DEPTH, LRU_BLOCKS, LRU_BW, LRU_BW), LRU_BW ** -0.5),
        'b_ix': nrm(ks[14], (DEPTH, LRU_WIDTH), 0.01),
        'lru_lambda': jnp.log(a0) - jnp.log1p(-a0),
        'w_out': nrm(ks[16], (DEPTH, MIX_WIDTH, D_MODEL), MIX_WIDTH ** -0.5),
        'norm2_g': 1.0 + nrm(ks[17], (DEPTH, D_MODEL), 0.02),
        'ffn_w1': nrm(ks[18], (N_DENSE, D_MODEL, D_FF), D_MODEL ** -0.5),
        'ffn_w3': nrm(ks[19], (N_DENSE, D_MODEL, D_FF), D_MODEL ** -0.5),
        'ffn_w2': nrm(ks[20], (N_DENSE, D_FF, D_MODEL), D_FF ** -0.5),
        'router_w': nrm(ks[21], (N_MOE, D_MODEL, N_EXPERTS), D_MODEL ** -0.5),
        'moe_w1': nrm(ks[22], (N_MOE, N_EXPERTS, D_MODEL, D_FF_EXPERT), D_MODEL ** -0.5),
        'moe_w3': nrm(ks[23], (N_MOE, N_EXPERTS, D_MODEL, D_FF_EXPERT), D_MODEL ** -0.5),
        'moe_w2': nrm(ks[24], (N_MOE, N_EXPERTS, D_FF_EXPERT, D_MODEL), D_FF_EXPERT ** -0.5),
        'final_norm_g': 1.0 + nrm(ks[25], (D_MODEL,), 0.02),
    }

def reference(x_prompt, x_sample, state_hgrn, state_lru, state_conv, norm1_g, w_in, lower_bounds,
              hg_norm_g, conv_w, conv_b, w_ra, b_ra, w_ix, b_ix, lru_lambda, w_out, norm2_g,
              ffn_w1, ffn_w3, ffn_w2, router_w, moe_w1, moe_w3, moe_w2, final_norm_g):
    params = (norm1_g, w_in, lower_bounds, hg_norm_g, conv_w, conv_b, w_ra, b_ra, w_ix, b_ix,
              lru_lambda, w_out, norm2_g, ffn_w1, ffn_w3, ffn_w2, router_w, moe_w1, moe_w3,
              moe_w2, final_norm_g)
    bp = x_prompt.shape[0]
    z_hg = jnp.zeros((DEPTH, bp, HG_HEADS, HG_DK, HG_DV), state_hgrn.dtype)
    z_lru = jnp.zeros((DEPTH, bp, LRU_WIDTH), state_lru.dtype)
    z_conv = jnp.zeros((DEPTH, bp, CONV_K - 1, LRU_WIDTH), state_conv.dtype)
    y_prompt, hg_p, lru_p, conv_p = trunk(x_prompt, z_hg, z_lru, z_conv, *params)
    y_sample, hg_s, lru_s, conv_s = trunk(x_sample, state_hgrn, state_lru, state_conv, *params)
    return (y_prompt, y_sample, hg_p, lru_p, conv_p, hg_s, lru_s, conv_s)


_drawn_inputs = setup_inputs


def setup_inputs(seed=0):
    import zlib

    import numpy as np

    out = dict(_drawn_inputs(seed))
    spreads = {}
    factors = {'hg_norm_g': 3.025, 'b_ra': 26.184, 'b_ix': 17.41, 'final_norm_g': 7.863}
    for name, (base, spread) in spreads.items():
        noise = np.random.default_rng([zlib.crc32(name.encode()), seed]).standard_normal(out[name].shape)
        drawn = base * np.exp(spread * noise) if base else spread * noise
        out[name] = __import__('jax').numpy.asarray(drawn.astype(out[name].dtype))
    for name, factor in factors.items():
        out[name] = (out[name] * factor).astype(out[name].dtype)
    return out
```

```python
import concourse.bass as bass
from concourse import mybir
from contextlib import ExitStack

F32 = mybir.dt.float32
F32R = mybir.dt.float32r
I32 = mybir.dt.int32
ALU = mybir.AluOpType
ACT = mybir.ActivationFunctionType
AX = mybir.AxisListType

D, P = 1024, 128
DC = D // P
DEPTH = 2
NPROMPT, NSAMPLE = 256, 8
T = NPROMPT + NSAMPLE
HEADS = 4
TAPS = 4
D_FF, D_FFE, EXPERTS = 2816, 3584, 8
EPS = 1e-6
MERGE_ORDER = [4, 5, 6, 7, 0, 1, 2, 3]
SLOTS = P
PRODUCTS = 17
START = 1
NORM_BANK = [4, 4, 0, 4, 4]
TINY, LN_TINY = 1e-19, -43.74911676688687

TOKEN_TILES = [(0, 0, 128), (1, 128, 128), (2, 256, 8)]

RAW, SPLIT = 6, 3
UNIT = 2048
IN_UNITS, OUT_UNITS = 12, 4
FF_STEPS = D_FF // 256
EX_STEPS = D_FFE // 512
IN_BASE = [0, IN_UNITS + OUT_UNITS + 3 * FF_STEPS]
OUT_BASE = [b + IN_UNITS for b in IN_BASE]
FF_BASE = OUT_BASE[0] + OUT_UNITS
EX_BASE = OUT_BASE[1] + OUT_UNITS
EX_UNITS = 6 * EX_STEPS
IN_COLS = [512, 0, 1024, 2048, 2560, 1536]

V_N1, V_N2, V_NF, V_LB, V_HG, V_CW, V_CB, V_RA, V_IX, V_LAM, V_ROWS = (
    0, 16, 32, 40, 48, 56, 88, 96, 104, 112, 120)
V_SLRU, V_SCONV, V_COLS = 128, 192, 384

O_LRUP, O_CONVP, O_LRUS, O_XRS, O_COLS = 0, 4, 16, 48, 80


def trunk(nc, x_prompt, x_sample, state_hgrn, state_lru, state_conv, norm1_g, w_in, lower_bounds,
          hg_norm_g, conv_w, conv_b, w_ra, b_ra, w_ix, b_ix, lru_lambda, w_out, norm2_g,
          ffn_w1, ffn_w3, ffn_w2, router_w, moe_w1, moe_w3, moe_w2, final_norm_g,
          y_prompt, y_sample, hgrn_prompt, lru_prompt, conv_prompt,
          hgrn_sample, lru_sample, conv_sample):
    ctx = ExitStack()
    with ctx:
        base0 = (nc.sbuf_base + 31) // 32 * 32
        slab_bytes = (nc.sbuf_usable_end - base0 - 64) // 32 * 32
        ctx.enter_context(nc.sbuf_tensor("slab", [P, slab_bytes // 4], F32))
        places = {}

        def at(name, offset, shape, dt=F32):
            size = 4
            for n in shape:
                size *= n
            assert offset % 32 == 0 and offset + size <= slab_bytes, (name, offset, size)
            places[name] = offset + (size + 31) // 32 * 32
            return nc.alloc_sbuf_tensor_at(name, [P] + list(shape), dt, offset=base0 + offset)

        def end(name):
            return places[name]

        raw = at("raw", 0, [RAW, UNIT])
        w_hi = at("w_hi", end("raw"), [SPLIT, UNIT], F32R)
        w_lo = at("w_lo", end("w_hi"), [SPLIT, UNIT], F32R)
        xT = at("xT", end("w_lo"), [DC, T])
        ident = at("ident", end("xT"), [P])
        ones = at("ones", end("ident"), [P])
        iota = at("iota", end("ones"), [P])
        before = at("before", end("iota"), [P])
        masks = at("masks", end("before"), [7, P], I32)
        vecT = at("vecT", end("masks"), [V_COLS])
        gate_w = at("gate_w", end("vecT"), [DEPTH, 2, HEADS, P])
        rw = at("rw", end("gate_w"), [DC, EXPERTS])
        small = at("small", end("rw"), [160])
        HH = end("small")
        h_hi = at("h_hi", HH, [DC, T], F32R)
        h_lo = at("h_lo", end("h_hi"), [DC, T], F32R)
        hstate = at("hstate", HH, [NSAMPLE * HEADS, P])
        WORK = end("h_lo")
        zq = at("zq", WORK, [HEADS, T])
        zf = at("zf", end("zq"), [HEADS, T])
        zv = at("zv", end("zf"), [HEADS, T])
        zg = at("zg", end("zv"), [HEADS, T])
        zx = at("zx", end("zg"), [HEADS, 3 + NPROMPT + 1])
        zr = at("zr", end("zx"), [HEADS, T])
        forget = at("forget", end("zr"), [HEADS, T])
        key = at("key", end("forget"), [HEADS, T])
        cum = at("cum", end("key"), [HEADS, T])
        lev = [at("lev0", end("cum"), [HEADS, T])]
        lev.append(at("lev1", end("lev0"), [HEADS, T]))
        lev.append(at("lev2", end("lev1"), [HEADS, T]))
        sc = at("sc", end("lev2"), [3, HEADS, P])
        v_tok = at("v_tok", end("sc"), [2, HEADS, P])
        k_tok = at("k_tok", end("v_tok"), [2, HEADS, P])
        v_diag = at("v_diag", end("v_tok"), [2, HEADS, P])
        oT = at("oT", end("k_tok"), [HEADS, T])
        s_fin = at("s_fin", end("oT"), [HEADS, P])
        outs = at("outs", end("s_fin"), [O_COLS])
        outs_t = at("outs_t", end("outs"), [P])
        vec_rows = at("vec_rows", end("lev2"), [4, P])
        xor_st = at("xor_st", end("vec_rows"), [4, P], I32)
        xor_f = at("xor_f", end("xor_st"), [2, P])
        sq = at("sq", WORK, [DC, T])
        hF = at("hF", end("sq"), [DC, T])
        rstd = at("rstd", end("hF"), [2, T])
        x_rows = at("x_rows", end("rstd"), [3, D])
        ff_silu = at("ff_silu", end("rstd"), [2, T])
        ff_g = at("ff_g", end("ff_silu"), [2, T])
        ff_hi = at("ff_hi", end("ff_g"), [2, 2, T], F32R)
        ff_lo = at("ff_lo", end("ff_hi"), [2, 2, T], F32R)
        h_tok = at("h_tok", end("hF"), [2, 3, D], F32R)
        xg = at("xg", end("h_tok"), [2, DC, P], F32R)
        pick = at("pick", end("xg"), [3, P], F32R)
        pickT = at("pickT", end("pick"), [T], F32R)
        ex_silu = at("ex_silu", end("pickT"), [512])
        ex_g = at("ex_g", end("ex_silu"), [512])
        gT = at("gT", end("ex_g"), [2, 4, P], F32R)
        y_ex = at("y_ex", end("gT"), [2, D], F32R)
        y_f = at("y_f", end("y_ex"), [D])
        rt = at("rt", HH, [16, 3, EXPERTS])
        blocks_i = at("blocks_i", end("rt"), [8], I32)
        place = at("place", end("blocks_i"), [3, EXPERTS + 1])
        y_rows = at("y_rows", end("hF"), [3, D])

        ps = ctx.enter_context(nc.psum_tensor("ps", [P, 8, 512], F32))

        eps = small[:, 0:1]
        lbv = small[:, 1:9]
        omlb = small[:, 9:17]
        crate = small[:, 17:25]
        ncrate = small[:, 25:33]
        rank = small[:, 33:41]
        valid = small[:, 41:44]
        gslot = small[:, 44:45]
        tmp = small[:, 48:160]

        names = {}

        def sem(name):
            names[name] = ctx.enter_context(nc.semaphore(name))
            return names[name]

        landed = [sem(f"landed{i}") for i in range(RAW)]
        hi_made = sem("hi_made")
        split = sem("split")
        used = sem("used")
        x_landed, vec_landed, gw_landed = sem("x_landed"), sem("vec_landed"), sem("gw_landed")
        rw_landed = sem("rw_landed")
        consts = sem("consts")
        pool_step, dve_step, act_step = sem("pool_step"), sem("dve_step"), sem("act_step")
        x_turned, vec_turned, vec_ready = sem("x_turned"), sem("vec_turned"), sem("vec_ready")
        x_sum = sem("x_sum")
        sq_ready, ssq_done, root_done = sem("sq_ready"), sem("ssq_done"), sem("root_done")
        h_full, h_hi_made, h_split = sem("h_full"), sem("h_hi_made"), sem("h_split")
        z_done, z_free = sem("z_done"), sem("z_free")
        f_sig, q_sig, g_sig, gelu_in, gelu_sig = (sem("f_sig"), sem("q_sig"), sem("g_sig"),
                                                  sem("gelu_in"), sem("gelu_sig"))
        f_ready, q_ready = sem("f_ready"), sem("q_ready")
        clamp_ready, ln_ready = sem("clamp_ready"), sem("ln_ready")
        lev_in, lev_exp, lev_ready = sem("lev_in"), sem("lev_exp"), sem("lev_ready")
        sc_done, sc_taken = sem("sc_done"), sem("sc_taken")
        v_turned, v_ready = sem("v_turned"), sem("v_ready")
        kd_in, kd_exp, kd_ready, kd_turned, kd_tok_ready = (
            sem("kd_in"), sem("kd_exp"), sem("kd_ready"), sem("kd_turned"), sem("kd_tok_ready"))
        fin_done, fin_ready, fin_stored = sem("fin_done"), sem("fin_ready"), sem("fin_stored")
        st_landed, st_decayed, diag_ready = sem("st_landed"), sem("st_decayed"), sem("diag_ready")
        kv_done, st_new, st_stored = sem("kv_done"), sem("st_new"), sem("st_stored")
        o_done, o_ready, o_sq, o_ssq, o_root = (sem("o_done"), sem("o_ready"), sem("o_sq"),
                                                sem("o_ssq"), sem("o_root"))
        conv_ready, gates_done, gates_ready = (sem("conv_ready"), sem("gates_done"),
                                               sem("gates_ready"))
        decay_ready, om_ready, om_root = sem("decay_ready"), sem("om_ready"), sem("om_root")
        merged, m_hi_made, m_split = sem("merged"), sem("m_hi_made"), sem("m_split")
        rows_in, rows_turned, rows_ready, rows_stored = (sem("rows_in"), sem("rows_turned"),
                                                         sem("rows_ready"), sem("rows_stored"))
        setup_in, setup_exp, pos_moved = sem("setup_in"), sem("setup_exp"), sem("pos_moved")
        ff_silu_done, ff_g_done, ff_hi_done, ff_split = (sem("ff_silu_done"), sem("ff_g_done"),
                                                         sem("ff_hi_done"), sem("ff_split"))
        y_done = sem("y_done")
        logits_done, margin_ready, margin_exp = (sem("logits_done"), sem("margin_ready"),
                                                 sem("margin_exp"))
        chosen_ready, pos_done, blocks_ready = (sem("chosen_ready"), sem("pos_done"),
                                                sem("blocks_ready"))
        ht_zero, ht_turned, ht_hi, ht_split = (sem("ht_zero"), sem("ht_turned"), sem("ht_hi"),
                                               sem("ht_split"))
        pick_ready, gathered, xg_hi, xg_lo = (sem("pick_ready"), sem("gathered"), sem("xg_hi"),
                                              sem("xg_lo"))
        pickT_done, pickT_ready = sem("pickT_done"), sem("pickT_ready")
        silu_done, g_done, g_turned, gT_hi, gT_split = (sem("silu_done"), sem("g_done"),
                                                        sem("g_turned"), sem("gT_hi"),
                                                        sem("gT_split"))
        y_gated, y_hi, y_split, spread, added = (sem("y_gated"), sem("y_hi"), sem("y_split"),
                                                 sem("spread"), sem("added"))
        yt_turned, yt_ready, stored = sem("yt_turned"), sem("yt_ready"), sem("stored")

        def unit_of(base, i=0):
            return base % RAW, base % SPLIT, 16 * (base // RAW + 1) + 16 * i, base + RAW * i

        block = ctx.enter_context(nc.Block())

        @block.sync
        def _(sp):
            def load(base, src, i=0, first=False):
                slot, _, _, u = unit_of(base, i)
                if not first:
                    sp.wait_ge(split, u - RAW + 1)
                shape = list(src.shape)
                dst = raw[:, slot, :].rearrange("p (c n) -> p c n", c=shape[1])
                sp.dma_start(dst, src).then_inc(landed[slot], 16)

            sp.dma_start(x_rows[:, 0:2, :], x_prompt.rearrange("a (t p) d -> p (a t) d", p=P)
                         ).then_inc(x_landed, 16)
            sp.dma_start(x_rows[0:NSAMPLE, 2, :], x_sample.rearrange("b s d -> (b s) d")
                         ).then_inc(x_landed, 16)

            def columns(w, n0, n=256):
                return w.rearrange("(c p) n -> p c n", p=P)[:, :, n0:n0 + n]

            def load_in(l):
                for u in range(IN_UNITS):
                    load(IN_BASE[l] + u, columns(w_in[l], IN_COLS[u // 2] + 256 * (u % 2)),
                         first=IN_BASE[l] + u < RAW)
                for u in range(OUT_UNITS):
                    load(OUT_BASE[l] + u, columns(w_out[l], 256 * u))

            load_in(0)
            load(FF_BASE, columns(ffn_w1[0], 0))
            load(FF_BASE + 1, columns(ffn_w3[0], 0))
            with sp.Fori(0, (FF_STEPS - 1) // 2) as i:
                for k in range(2):
                    n0 = i * 512 + 256 * (k + 1)
                    r0 = i * 512 + 256 * k
                    w1c = ffn_w1[0].rearrange("(c p) n -> p c n", p=P)
                    w3c = ffn_w3[0].rearrange("(c p) n -> p c n", p=P)
                    w2r = ffn_w2[0].rearrange("(j p) n -> p j n", p=P)
                    load(FF_BASE + 2 + 3 * k, w1c[:, :, bass.ds(n0, 256)], i)
                    load(FF_BASE + 3 + 3 * k, w3c[:, :, bass.ds(n0, 256)], i)
                    load(FF_BASE + 4 + 3 * k, w2r[:, bass.ds(i * 4 + 2 * k, 2), :], i)
            load(FF_BASE + 3 * FF_STEPS - 1,
                 ffn_w2[0].rearrange("(j p) n -> p j n", p=P)[:, 2 * FF_STEPS - 2:2 * FF_STEPS, :])
            load_in(1)
            ew1 = moe_w1[0].rearrange("e (c p) n -> p (e c) n", p=P)
            ew3 = moe_w3[0].rearrange("e (c p) n -> p (e c) n", p=P)
            ew2 = moe_w2[0].rearrange("e (j p) n -> p (e j) n", p=P)

            def load_up(base, e, n0, i):
                for k, w in enumerate((ew1, ew3)):
                    for half in range(2):
                        load(base + 2 * k + half,
                             w[:, bass.ds(e * DC + 4 * half, 4), bass.ds(n0, 512)], i)

            def load_down(base, e, s, i):
                for half in range(2):
                    load(base + half,
                         ew2[:, bass.ds(e * (4 * EX_STEPS) + s * 4 + 2 * half, 2), :], i)

            def expert(b, e):
                it = (b * EXPERTS + e) * EX_STEPS
                load_up(EX_BASE, e, 0, it)
                with sp.Fori(1, EX_STEPS) as s:
                    load_up(EX_BASE + 4, e, s * 512, it + s - 1)
                    load_down(EX_BASE + 8, e, s - 1, it + s - 1)
                load_down(EX_BASE + 4 + 6 * (EX_STEPS - 1), e, EX_STEPS - 1, it)

            with sp.Fori(0, EXPERTS) as e:
                expert(0, e)
            sp.wait_ge(blocks_ready, 1)
            nb = sp.value_load(blocks_i[0:1, 0:1], min_val=1, max_val=3)
            with sp.If(nb > 1):
                with sp.Fori(1, nb) as b:
                    with sp.Fori(0, EXPERTS) as e:
                        expert(b, e)

        @block.gpsimd
        def _(pool):
            steps = [0]

            def link(ins):
                steps[0] += 1
                ins.then_inc(pool_step, 1)
                pool.wait_ge(pool_step, steps[0])

            pool.memset(gate_w[:, :, :, :, :], 0.0).then_inc(pool_step, 1)
            pool.memset(ident[:, :], 0.0).then_inc(pool_step, 1)
            pool.memset(ones[:, :], 1.0).then_inc(pool_step, 1)
            pool.memset(valid, 1.0).then_inc(pool_step, 1)
            pool.memset(eps, EPS).then_inc(pool_step, 1)
            steps[0] = 5
            pool.wait_ge(pool_step, 5)
            link(pool.affine_select(out=ident[:, :], in_=ident[:, :], compare_op=ALU.not_equal,
                                    fill=1.0, base=0, pattern=[[-1, P]], channel_multiplier=1))
            pool.affine_select(out=before[:, :], in_=ones[:, :], compare_op=ALU.is_gt, fill=0.0,
                               base=0, pattern=[[1, P]], channel_multiplier=-1
                               ).then_inc(pool_step, 1)
            pool.affine_select(out=valid, in_=valid, compare_op=ALU.is_gt, fill=0.0, base=T,
                               pattern=[[-P, 3]], channel_multiplier=-1).then_inc(pool_step, 1)
            pool.iota(iota[:, :], pattern=[[1, P]], base=0, channel_multiplier=0,
                      allow_small_or_imprecise_dtypes=True).then_inc(pool_step, 1)
            pool.iota(rank, pattern=[[-1, EXPERTS]], base=EXPERTS, channel_multiplier=0,
                      allow_small_or_imprecise_dtypes=True).then_inc(pool_step, 1)
            pool.iota(xor_st[:, 0, :], pattern=[[0, P]], base=0, channel_multiplier=1
                      ).then_inc(pool_step, 1)
            pool.iota(xor_st[:, 1, :], pattern=[[1, P]], base=0, channel_multiplier=0
                      ).then_inc(pool_step, 1)
            steps[0] += 6
            pool.wait_ge(pool_step, steps[0])
            pool.sem_inc(consts, 1)
            for l in range(DEPTH):
                for k, w in enumerate((w_ra, w_ix)):
                    for half in range(2):
                        rows = slice(64 * half, 64 * half + 64)
                        pool.dma_start(gate_w[rows, l, k, :, rows],
                                       w[l].rearrange("(j two) c d -> two c j d", two=2)[half]
                                       ).then_inc(gw_landed, 16)
            pool.dma_start(rw[:, :, :], router_w[0].rearrange("(c p) e -> p c e", p=P)
                           ).then_inc(rw_landed, 16)
            pool.dma_start(conv_sample[:, :, 0:2, :], state_conv[:, :, 1:3, :]
                           ).then_inc(rows_stored, 16)

            for l in range(DEPTH):
                pool.wait_ge(used, IN_BASE[l] + IN_UNITS)
                pool.dma_start(hstate[:, :, :], state_hgrn[l].rearrange("b h k v -> k (b h) v")
                               ).then_inc(st_landed, 16)
                pool.wait_ge(st_landed, 16 * (l + 1))
                pool.wait_ge(f_ready, l + 1)
                fs = forget[:, :, NPROMPT:T].rearrange("p h b -> p b h")
                for b in range(NSAMPLE):
                    f_b = forget[:, :, NPROMPT + b:NPROMPT + b + 1].broadcast_to([P, HEADS, P])
                    st = hstate[:, HEADS * b:HEADS * (b + 1), :]
                    pool.tensor_tensor(st, st, f_b, ALU.mult).then_inc(st_decayed, 1)
                pool.wait_ge(fin_done, l + 1)
                for b in range(NSAMPLE):
                    if b >= 2:
                        pool.wait_ge(kv_done, NSAMPLE * l + b - 1)
                    v_b = zv[:, :, NPROMPT + b:NPROMPT + b + 1].broadcast_to([P, HEADS, P])
                    pool.tensor_tensor(v_diag[:, b % 2, :, :],
                                       ident[:, None, :].broadcast_to([P, HEADS, P]), v_b,
                                       ALU.mult).then_inc(diag_ready, 1)
                pool.wait_ge(st_new, NSAMPLE * HEADS * (l + 1))
                pool.dma_start(hgrn_sample[l].rearrange("b h k v -> k (b h) v"), hstate[:, :, :]
                               ).then_inc(st_stored, 16)
                pool.wait_ge(fin_ready, l + 1)
                pool.dma_start(hgrn_prompt[l, 0].rearrange("h k v -> k h v"), s_fin[:, :, :]
                               ).then_inc(fin_stored, 16)
                pool.wait_ge(rows_ready, l + 1)
                rows = lambda a, n: outs_t[a:a + n, :]
                pool.dma_start(lru_prompt[l].rearrange("a (j p) -> (a j) p", p=P),
                               rows(O_LRUP, 4)).then_inc(rows_stored, 16)
                pool.dma_start(conv_prompt[l].rearrange("a t (j p) -> (a t j) p", p=P),
                               rows(O_CONVP, 12)).then_inc(rows_stored, 16)
                pool.dma_start(lru_sample[l].rearrange("b (j p) -> (b j) p", p=P),
                               rows(O_LRUS, 32)).then_inc(rows_stored, 16)
                pool.dma_start(conv_sample[l, :, 2, :].rearrange("b (j p) -> b j p", p=P),
                               rows(O_XRS, 32)).then_inc(rows_stored, 16)
            pool.wait_ge(st_stored, 16 * DEPTH)
            pool.wait_ge(fin_stored, 16 * DEPTH)
            pool.wait_ge(rows_stored, 16 * (1 + 4 * DEPTH))

        @block.scalar
        def _(act):
            steps = [0]

            def link(ins):
                steps[0] += 1
                ins.then_inc(act_step, 1)
                act.wait_ge(act_step, steps[0])

            def hi(base, i=0):
                r, s, lands, u = unit_of(base, i)
                act.wait_ge(landed[r], lands)
                if not isinstance(u, int) or u >= SPLIT:
                    act.wait_ge(used, u - SPLIT + 1)
                act.activation(w_hi[:, s, :], raw[:, r, :], ACT.Copy).then_inc(hi_made, 1)

            vectors = ((norm1_g, V_N1, 16), (norm2_g, V_N2, 16), (final_norm_g, V_NF, 8),
                       (lower_bounds, V_LB, 8), (hg_norm_g, V_HG, 8), (conv_w, V_CW, 32),
                       (conv_b, V_CB, 8), (b_ra, V_RA, 8), (b_ix, V_IX, 8), (lru_lambda, V_LAM, 8))
            for v, r0, n in vectors:
                flat = {1: "(j p) -> j p", 2: "l (j p) -> (l j) p",
                        3: "l t (j p) -> (l t j) p"}[len(v.shape)]
                act.dma_start(vec_rows[r0:r0 + n, 0, :], v.rearrange(flat, p=P)
                              ).then_inc(vec_landed, 16)
            act.dma_start(vec_rows[0:64, 1, :], state_lru.rearrange("l b (j p) -> (l b j) p", p=P)
                          ).then_inc(vec_landed, 16)
            for l in range(DEPTH):
                act.dma_start(vec_rows[0:96, 2 + l, :],
                              state_conv[l].rearrange("b t (j p) -> (b t j) p", p=P)
                              ).then_inc(vec_landed, 16)
            act.sem_inc(z_free, 4)

            def norm(n, chunk_sum):
                for c in range(DC):
                    act.wait_ge(x_sum, chunk_sum(c))
                    act.activation(sq[:, c, :], xT[:, c, :], ACT.Square).then_inc(sq_ready, 1)
                act.wait_ge(ssq_done, n + 1)
                act.activation(rstd[:, 0, :], ps[:, NORM_BANK[n], 0:T], ACT.Sqrt, bias=eps, scale=1.0 / D
                               ).then_inc(root_done, 1)

            def norm_hi(n):
                for c in range(DC):
                    act.wait_ge(h_full, DC * n + c + 1)
                    act.activation(h_hi[:, c, :], hF[:, c, :], ACT.Copy).then_inc(h_hi_made, 1)

            def z_out(l, n):
                act.wait_ge(z_done, 24 * l + n + 1)
                bank, h = ps[:, n % 4, :], n % 4
                group = n // 4
                if group == 3:
                    act.activation(zx[:, h, 3:3 + NPROMPT], bank[:, 0:NPROMPT], ACT.Copy
                                   ).then_inc(act_step, 1)
                    steps[0] += 1
                    cols = outs[:, O_XRS:O_XRS + 32].rearrange("p (b j) -> p j b", j=HEADS)
                    act.activation(cols[:, h, :], bank[:, NPROMPT:T], ACT.Copy
                                   ).then_inc(z_free, 1)
                else:
                    dst = (zf, zq, zv, None, zr, zg)[group]
                    act.activation(dst[:, h, :], bank[:, 0:T], ACT.Copy).then_inc(z_free, 1)

            def mixer(l):
                ib, ob = IN_BASE[l], OUT_BASE[l]
                for u in range(IN_UNITS + SPLIT):
                    hi(ib + u)
                    if l == 0 and u == SPLIT - 1:
                        act.wait_ge(setup_in, 2)
                        act.activation(tmp[:, 8:16], tmp[:, 8:16], ACT.Exp).then_inc(setup_exp, 1)
                        act.activation(tmp[:, 24:32], tmp[:, 24:32], ACT.Exp
                                       ).then_inc(setup_exp, 1)
                    if u >= SPLIT:
                        z_out(l, 2 * (u - SPLIT))
                        z_out(l, 2 * (u - SPLIT) + 1)
                    zs = lambda n: act.wait_ge(z_free, 4 + 24 * l + n)
                    if u == SPLIT + 1:
                        zs(4)
                        act.activation(lev[0][:, :, :], zf[:, :, :], ACT.Sigmoid
                                       ).then_inc(f_sig, 1)
                        act.activation(lev[1][:, :, :], zf[:, :, :], ACT.Sigmoid, scale=-1.0
                                       ).then_inc(f_sig, 1)
                    if u == SPLIT + 3:
                        zs(8)
                        act.activation(oT[:, :, :], zq[:, :, :], ACT.Sigmoid).then_inc(q_sig, 1)
                        act.wait_ge(clamp_ready, l + 1)
                        act.activation(lev[0][:, :, :], lev[0][:, :, :], ACT.Ln
                                       ).then_inc(ln_ready, 1)
                act.wait_ge(v_turned, l + 1)
                act.activation(v_tok[:, :, :, :].rearrange("p c h v -> p (c h v)"),
                               ps[:, 6:8, :].rearrange("p a b -> p (a b)"), ACT.Copy
                               ).then_inc(v_ready, 1)
                for k in range(8):
                    act.wait_ge(lev_in, 8 * l + k + 1)
                    x = lev[k % 3][:, :, 0:NPROMPT]
                    act.activation(x, x, ACT.Exp).then_inc(lev_exp, 1)
                act.wait_ge(kd_in, l + 1)
                x = lev[2][:, :, 0:NPROMPT]
                act.activation(x, x, ACT.Exp).then_inc(kd_exp, 1)
                act.wait_ge(kd_turned, l + 1)
                act.activation(k_tok[:, :, :, :].rearrange("p c h v -> p (c h v)"),
                               ps[:, 6:8, :].rearrange("p a b -> p (a b)"), ACT.Copy
                               ).then_inc(kd_tok_ready, 1)
                act.wait_ge(fin_done, l + 1)
                if l:
                    act.wait_ge(fin_stored, 16 * l)
                act.activation(s_fin[:, :, :].rearrange("p h v -> p (h v)"), ps[:, 4, :],
                               ACT.Copy).then_inc(fin_ready, 1)
                act.wait_ge(z_free, 4 + 24 * (l + 1))
                act.activation(zf[:, :, :], zg[:, :, :], ACT.Sigmoid).then_inc(g_sig, 1)
                act.wait_ge(gelu_in, l + 1)
                act.activation(cum[:, :, :], cum[:, :, :], ACT.Sigmoid, scale=1.5957691216057308
                               ).then_inc(gelu_sig, 1)
                for n in range(8):
                    act.wait_ge(gates_done, 8 * l + n + 1)
                    j = n % 4
                    bias = vecT[:, (V_RA, V_IX)[n // 4] + 4 * l + j:][:, 0:1]
                    act.activation(lev[1 + n // 4][:, j, :], ps[:, 4 + j, 0:T], ACT.Sigmoid,
                                   bias=bias).then_inc(gates_ready, 1)
                act.wait_ge(gates_ready, 8 * (l + 1))
                act.wait_ge(g_sig, l + 1)
                for j in range(HEADS):
                    act.activation(key[:, j, :], lev[1][:, j, :], ACT.Tanh,
                                   scale=crate[:, 4 * l + j:4 * l + j + 1]
                                   ).then_inc(decay_ready, 1)
                act.wait_ge(decay_ready, 8 * l + 4)
                for j in range(HEADS):
                    link(act.activation(lev[1][:, j, :], lev[1][:, j, :], ACT.Exp,
                                        scale=ncrate[:, 4 * l + j:4 * l + j + 1]))
                    act.sem_inc(decay_ready, 1)
                act.wait_ge(om_ready, l + 1)
                act.activation(key[:, :, :], key[:, :, :], ACT.Sqrt).then_inc(om_root, 1)
                act.wait_ge(o_ready, l + 1)
                act.activation(zf[:, :, :], oT[:, :, :], ACT.Square).then_inc(o_sq, 1)
                act.wait_ge(o_ssq, l + 1)
                act.activation(zf[:, :, :], ps[:, 4:8, 0:T], ACT.Sqrt, bias=eps, scale=1.0 / P
                               ).then_inc(o_root, 1)
                act.wait_ge(st_stored, 16 * (l + 1))
                for n, c in enumerate(MERGE_ORDER):
                    act.wait_ge(merged, DC * l + n + 1)
                    src = oT[:, c, :] if c < HEADS else lev[0][:, c - HEADS, :]
                    act.activation(h_hi[:, c, :], src, ACT.Copy).then_inc(m_hi_made, 1)
                hi(ob + 3)

            norm(0, lambda c: c + 1)
            norm_hi(0)
            mixer(0)
            norm(1, lambda c: 8 + c + 1)
            norm_hi(1)
            hi(FF_BASE)
            hi(FF_BASE + 1)

            def ff_act(s, used_w1):
                act.wait_ge(used, used_w1)
                act.wait_ge(ff_g_done, s)
                act.activation(ff_silu[:, :, :], ps[:, 0:2, 0:T], ACT.Silu
                               ).then_inc(ff_silu_done, 1)

            def ff_high(s, parity):
                act.wait_ge(ff_g_done, s + 1)
                act.activation(ff_hi[:, parity, :, :], ff_g[:, :, :], ACT.Copy
                               ).then_inc(ff_hi_done, 1)

            ff_act(0, FF_BASE + 1)
            with act.Fori(0, (FF_STEPS - 1) // 2) as i:
                for k in range(2):
                    s = i * 2 + (k + 1)
                    b = FF_BASE + 2 + 3 * k
                    hi(b, i)
                    ff_high(s - 1, k)
                    hi(b + 1, i)
                    hi(b + 2, i)
                    ff_act(s, i * RAW + (b + 1))
            ff_high(FF_STEPS - 1, 0)
            hi(FF_BASE + 3 * FF_STEPS - 1)
            norm(2, lambda c: 16 + 8 * (FF_STEPS - 1) + c + 1)
            norm_hi(2)
            mixer(1)
            norm(3, lambda c: 16 + 8 * FF_STEPS + c + 1)
            act.wait_ge(margin_ready, 1)
            act.activation(rt[:, 9, :, 0], rt[:, 8, :, 0], ACT.Exp).then_inc(margin_exp, 1)
            for n in range(6):
                t, half = n // 2, n % 2
                rows = TOKEN_TILES[t][2]
                act.wait_ge(ht_turned, n + 1)
                if n == 0:
                    act.wait_ge(ht_zero, 1)
                act.activation(h_tok[0:rows, 0, t, 512 * half:512 * half + 512],
                               ps[0:rows, 2 + half, :], ACT.Copy).then_inc(ht_hi, 1)

            def gather_high(it):
                for half in range(2):
                    act.wait_ge(gathered, it * 4 + (half + 1))
                    act.activation(xg[:, 0, 4 * half:4 * half + 4, :],
                                   ps[:, 5 + half, :].rearrange("p (c n) -> p c n", c=4),
                                   ACT.Copy).then_inc(xg_hi, 1)

            def y_high(it):
                act.wait_ge(y_gated, it * 2 + 2)
                act.wait_ge(spread, START + it * DC)
                act.activation(y_ex[:, 0, :], y_f[:, :], ACT.Copy).then_inc(y_hi, 1)

            gather_high(0)
            act.wait_ge(blocks_ready, 1)
            nb = act.value_load(blocks_i[0:1, 0:1], min_val=1, max_val=3)
            with act.Fori(0, nb) as b:
                with act.Fori(0, EXPERTS) as e:
                    it = b * EXPERTS + e
                    s0 = it * EX_STEPS
                    for j in range(3):
                        hi(EX_BASE + j, s0)
                    y_high(it)
                    hi(EX_BASE + 3, s0)

                    def silu(s, w1_used):
                        act.wait_ge(used, w1_used)
                        act.wait_ge(g_done, START + s)
                        act.activation(ex_silu[:, :], ps[:, 0, :], ACT.Silu
                                       ).then_inc(silu_done, 1)

                    def turned_high(s):
                        act.wait_ge(g_turned, START + s + 1)
                        act.activation(gT[:, 0, :, :].rearrange("p j n -> p (j n)"), ps[:, 2, :],
                                       ACT.Copy).then_inc(gT_hi, 1)

                    silu(s0, s0 * RAW + (EX_BASE + 2))
                    with act.Fori(1, EX_STEPS) as s:
                        i = s0 + (s - 1)
                        for j in range(4):
                            hi(EX_BASE + 4 + j, i)
                        turned_high(i)
                        silu(i + 1, i * RAW + (EX_BASE + 6))
                        hi(EX_BASE + 8, i)
                        hi(EX_BASE + 9, i)
                    hi(EX_BASE + EX_UNITS - 2, s0)
                    hi(EX_BASE + EX_UNITS - 1, s0)
                    gather_high(it + 1)
                    turned_high(s0 + (EX_STEPS - 1))
            y_high(nb * EXPERTS)
            norm(4, lambda c: 16 + 8 * FF_STEPS + 8 + 1)
            for t, t0, n in TOKEN_TILES:
                act.wait_ge(yt_ready, 2 * t + 2)
                dst = (y_prompt[0, t0:t0 + n, :] if t < 2 else
                       y_sample.rearrange("b s d -> (b s) d"))
                act.dma_start(dst, y_rows[0:n, t, :]).then_inc(stored, 16)
            act.wait_ge(stored, 48)

        @block.vector
        def _(dve):
            steps = [0]

            def link(ins):
                steps[0] += 1
                ins.then_inc(dve_step, 1)
                dve.wait_ge(dve_step, steps[0])

            def lo(base, i=0):
                r, s, _, u = unit_of(base, i)
                dve.wait_ge(hi_made, u + 1)
                dve.tensor_tensor(w_lo[:, s, :], raw[:, r, :], w_hi[:, s, :].bitcast(F32),
                                  ALU.subtract).then_inc(split, 1)

            def bc(ap, n):
                return ap.broadcast_to([P, HEADS, n])

            for c in range(DC):
                dve.wait_ge(x_turned, c + 1)
                dve.tensor_copy(xT[:, c, :], ps[:, c % 4, 0:T]).then_inc(x_sum, 1)
            dve.wait_ge(vec_turned, 1)
            link(dve.tensor_copy(vecT[:, 0:V_ROWS], ps[:, 5, 0:V_ROWS]))
            link(dve.tensor_copy(vecT[:, V_SLRU:V_COLS], ps[:, 5, V_SLRU:V_COLS]))
            dve.sem_inc(vec_ready, 1)

            def norm(n, gain, split_it=True):
                dve.wait_ge(root_done, n + 1)
                link(dve.reciprocal(rstd[:, 1, :], rstd[:, 0, :]))
                for c in range(DC):
                    dve.scalar_tensor_tensor(out=hF[:, c, :], in0=xT[:, c, :],
                                             scalar=vecT[:, gain + c:gain + c + 1],
                                             in1=rstd[:, 1, :], op0=ALU.mult, op1=ALU.mult
                                             ).then_inc(h_full, 1)

            def norm_lo(n):
                for c in range(DC):
                    dve.wait_ge(h_hi_made, DC * n + c + 1)
                    dve.tensor_tensor(h_lo[:, c, :], hF[:, c, :], h_hi[:, c, :].bitcast(F32),
                                      ALU.subtract).then_inc(h_split, 1)

            def setup():
                a, b = vecT[:, V_LB:V_LB + 4], vecT[:, V_LB + 4:V_LB + 8]
                t = lambda k: tmp[:, 8 * k:8 * k + 8]
                link(dve.tensor_tensor(t(0)[:, 0:4], a, b, ALU.max))
                link(dve.tensor_tensor(t(1)[:, 0:4], a, t(0)[:, 0:4], ALU.subtract))
                dve.tensor_tensor(t(1)[:, 4:8], b, t(0)[:, 0:4], ALU.subtract
                                  ).then_inc(setup_in, 1)
                lam = vecT[:, V_LAM:V_LAM + 8]
                link(dve.tensor_scalar(t(2), lam, -1.0, None, ALU.mult))
                dve.tensor_tensor(t(3), lam, t(2), ALU.min).then_inc(setup_in, 1)
                dve.wait_ge(setup_exp, 2)
                link(dve.tensor_tensor(t(5)[:, 0:4], t(1)[:, 0:4], t(1)[:, 4:8], ALU.add))
                link(dve.reciprocal(t(5)[:, 0:4], t(5)[:, 0:4]))
                link(dve.memset(lbv[:, 0:4], 0.0))
                link(dve.tensor_tensor(lbv[:, 4:8], t(1)[:, 4:8], t(5)[:, 0:4], ALU.mult))
                link(dve.tensor_scalar(omlb, lbv, -1.0, 1.0, ALU.mult, ALU.add))
                link(dve.tensor_scalar(t(5), t(3), 2.0, None, ALU.add))
                link(dve.reciprocal(t(5), t(5)))
                link(dve.tensor_tensor(t(3), t(3), t(5), ALU.mult))
                link(dve.tensor_tensor(t(5), t(3), t(3), ALU.mult))
                link(dve.memset(t(6), 1.0 / 19))
                for k in range(17, 0, -2):
                    link(dve.tensor_tensor(t(6), t(6), t(5), ALU.mult))
                    link(dve.tensor_scalar(t(6), t(6), 1.0 / k, None, ALU.add))
                link(dve.tensor_tensor(t(6), t(6), t(3), ALU.mult))
                link(dve.tensor_scalar(t(2), t(2), 0.0, None, ALU.max))
                link(dve.scalar_tensor_tensor(out=t(2), in0=t(6), scalar=2.0, in1=t(2),
                                              op0=ALU.mult, op1=ALU.add))
                link(dve.tensor_scalar(crate, t(2), 8.0, None, ALU.mult))
                link(dve.tensor_scalar(ncrate, t(2), -8.0, None, ALU.mult))
                dve.wait_ge(consts, 1)
                link(dve.tensor_tensor(xor_st[:, 2, :], xor_st[:, 0, :], xor_st[:, 1, :],
                                       ALU.bitwise_xor))
                link(dve.tensor_tensor(xor_f[:, 0, :], xor_st[:, 2, :], before[:, :], ALU.mult))
                for k in range(7):
                    link(dve.tensor_scalar(xor_f[:, 1, :], xor_f[:, 0, :], float(1 << k), None,
                                           ALU.is_ge))
                    link(dve.scalar_tensor_tensor(out=masks[:, k, :], in0=xor_f[:, 0, :],
                                                  scalar=float(2 << k), in1=xor_f[:, 1, :],
                                                  op0=ALU.is_lt, op1=ALU.mult))

            def mixer(l):
                ib, ob = IN_BASE[l], OUT_BASE[l]
                v = lambda col: vecT[:, col:col + 1]
                dve.wait_ge(x_sum, 8 if l == 0 else 16 + 8 * FF_STEPS)
                link(dve.memset(zx[:, :, 0:3], 0.0))

                def forget_and_key():
                    dve.wait_ge(f_sig, 2 * l + 2)
                    for h in range(HEADS):
                        k = 4 * l + h
                        link(dve.tensor_scalar(key[:, h, :], lev[1][:, h, :], omlb[:, k:k + 1],
                                               None, ALU.mult))
                        link(dve.tensor_scalar(forget[:, h, :], lev[0][:, h, :],
                                               omlb[:, k:k + 1], lbv[:, k:k + 1],
                                               ALU.mult, ALU.add))
                    dve.sem_inc(f_ready, 1)
                    dve.tensor_scalar(lev[0][:, :, :], forget[:, :, :], TINY, None, ALU.max
                                      ).then_inc(clamp_ready, 1)
                    link(dve.tensor_scalar(lev[1][:, :, :], forget[:, :, :], TINY, None,
                                           ALU.is_lt))
                    link(dve.scalar_tensor_tensor(out=lev[1][:, :, :], in0=zf[:, :, :],
                                                  scalar=-LN_TINY, in1=lev[1][:, :, :],
                                                  op0=ALU.add, op1=ALU.mult))

                def log_forget():
                    dve.wait_ge(q_sig, l + 1)
                    dve.tensor_tensor(zq[:, :, :], zq[:, :, :], oT[:, :, :], ALU.mult
                                      ).then_inc(q_ready, 1)
                    dve.wait_ge(ln_ready, l + 1)
                    link(dve.tensor_tensor(lev[0][:, :, :], lev[0][:, :, :], lev[1][:, :, :],
                                           ALU.add))
                    link(dve.memset(lev[1][:, 0, 0:NPROMPT], 1.0))
                    for h in range(HEADS):
                        link(dve.tensor_tensor_scan(cum[:, h, 0:NPROMPT],
                                                    lev[1][:, 0, 0:NPROMPT],
                                                    lev[0][:, h, 0:NPROMPT], 0.0, ALU.mult,
                                                    ALU.add))

                def level(k):
                    half, x = 1 << k, lev[k % 3]
                    if k >= 3:
                        dve.wait_ge(sc_done, PRODUCTS * l + (2 * (k - 3) + 4))
                    parts = lambda a: a[:, :, 0:NPROMPT].rearrange(
                        "p h (n two m) -> p h n two m", two=2, m=half)
                    cv, xv, qv, kv = parts(cum), parts(x), parts(zq), parts(key)
                    n = NPROMPT // (2 * half)
                    if k == 0:
                        dve.wait_ge(q_ready, l + 1)
                    for h4 in ([slice(0, 4)] if True else []):
                        mid = cv[:, :, :, 0, half - 1:half].broadcast_to([P, HEADS, n, half])
                        dve.tensor_tensor(xv[:, :, :, 0, :], mid, cv[:, :, :, 0, :],
                                          ALU.subtract).then_inc(dve_step, 1)
                        steps[0] += 1
                        dve.tensor_tensor(xv[:, :, :, 1, :], cv[:, :, :, 1, :], mid,
                                          ALU.subtract).then_inc(dve_step, 1)
                        steps[0] += 1
                    dve.wait_ge(dve_step, steps[0])
                    dve.sem_inc(lev_in, 1)

                def level_finish(k):
                    half, x = 1 << k, lev[k % 3]
                    parts = lambda a: a[:, :, 0:NPROMPT].rearrange(
                        "p h (n two m) -> p h n two m", two=2, m=half)
                    xv, qv, kv = parts(x), parts(zq), parts(key)
                    dve.wait_ge(lev_exp, 8 * l + k + 1)
                    dve.tensor_tensor(xv[:, :, :, 0, :], xv[:, :, :, 0, :], kv[:, :, :, 0, :],
                                      ALU.mult).then_inc(lev_ready, 1)
                    dve.tensor_tensor(xv[:, :, :, 1, :], xv[:, :, :, 1, :], qv[:, :, :, 1, :],
                                      ALU.mult).then_inc(lev_ready, 1)

                for u in range(IN_UNITS + SPLIT):
                    lo(ib + u)
                    if l == 0 and u == SPLIT - 1:
                        setup()
                    if u == SPLIT + 1:
                        forget_and_key()
                    if u == SPLIT + 3:
                        log_forget()

                def take(n, c, k):
                    dve.wait_ge(sc_done, PRODUCTS * l + n + 1)
                    bank = ps[:, n % 4, :].rearrange("p (h t) -> p h t", h=HEADS)
                    if k is None:
                        ins = dve.tensor_tensor(sc[:, c, :, :], bank, bc(ident[:, None, :], P),
                                                ALU.mult)
                    elif k == 7:
                        ins = dve.tensor_copy(sc[:, c, :, :], bank)
                    else:
                        ins = dve.copy_predicated(sc[:, c, :, :], bc(masks[:, k:k + 1, :], P),
                                                  bank)
                    ins.then_inc(sc_taken, 1)

                level(0)
                level(1)
                for k in range(8):
                    level_finish(k)
                    if k + 2 < 8:
                        level(k + 2)
                    if k == 1:
                        take(0, 0, None)
                        take(1, 1, None)
                        dve.wait_ge(sc_taken, PRODUCTS * l + 2)
                    if k >= 1:
                        take(2 * k, 0, k - 1)
                        take(2 * k + 1, 1, k - 1)
                        dve.wait_ge(sc_taken, PRODUCTS * l + 2 * k + 2)
                take(16, 2, 7)
                x = lev[2][:, :, 0:NPROMPT]
                dve.wait_ge(sc_done, PRODUCTS * l + 17)
                link(dve.tensor_tensor(x, bc(cum[:, :, NPROMPT - 1:NPROMPT], NPROMPT),
                                       cum[:, :, 0:NPROMPT], ALU.subtract))
                dve.sem_inc(kd_in, 1)
                dve.wait_ge(kd_exp, l + 1)
                link(dve.tensor_tensor(x, x, key[:, :, 0:NPROMPT], ALU.mult))
                dve.sem_inc(kd_ready, 1)

                xc = lev[0]
                for j in range(HEADS):
                    link(dve.tensor_scalar(xc[:, j, 0:NPROMPT], zx[:, j, 0:NPROMPT],
                                           v(V_CW + 16 * l + j), v(V_CB + 4 * l + j),
                                           ALU.mult, ALU.add))
                    for tap in range(1, TAPS):
                        link(dve.scalar_tensor_tensor(
                            out=xc[:, j, 0:NPROMPT], in0=zx[:, j, tap:tap + NPROMPT],
                            scalar=v(V_CW + 16 * l + 4 * tap + j), in1=xc[:, j, 0:NPROMPT],
                            op0=ALU.mult, op1=ALU.add))
                xs = outs[:, O_XRS:O_XRS + 32].rearrange("p (b j) -> p j b", j=HEADS)
                old = vecT[:, V_SCONV + 96 * l:V_SCONV + 96 * l + 96].rearrange(
                    "p (b t j) -> p t j b", t=3, j=HEADS)
                xcs, part = xc[:, :, NPROMPT:T], tmp[:, 0:32].rearrange("p (j b) -> p j b", j=4)
                for tap in range(TAPS):
                    w = bc(vecT[:, V_CW + 16 * l + 4 * tap:V_CW + 16 * l + 4 * tap + 4, None], 8)
                    src = old[:, tap] if tap < 3 else xs
                    link(dve.tensor_tensor(part if tap else xcs, src, w, ALU.mult))
                    if tap:
                        link(dve.tensor_tensor(xcs, xcs, part, ALU.add))
                link(dve.tensor_tensor(xcs, xcs, bc(vecT[:, V_CB + 4 * l:V_CB + 4 * l + 4, None],
                                                    8), ALU.add))
                dve.sem_inc(conv_ready, 1)
                cp = outs[:, O_CONVP:O_CONVP + 12].rearrange("p (t j) -> p j t", j=HEADS)
                link(dve.tensor_copy(cp, zx[:, :, NPROMPT:NPROMPT + 3]))

                link(dve.tensor_tensor(cum[:, :, :], zr[:, :, :], zr[:, :, :], ALU.mult))
                link(dve.tensor_scalar(cum[:, :, :], cum[:, :, :], 0.044715, 1.0, ALU.mult,
                                       ALU.add))
                link(dve.tensor_tensor(cum[:, :, :], cum[:, :, :], zr[:, :, :], ALU.mult))
                dve.sem_inc(gelu_in, 1)

                for b in range(NSAMPLE):
                    dve.wait_ge(kv_done, NSAMPLE * l + b + 1)
                    dve.wait_ge(st_decayed, NSAMPLE * l + b + 1)
                    for h in range(HEADS):
                        st = hstate[:, HEADS * b + h, :]
                        dve.scalar_tensor_tensor(
                            out=st, in0=ps[:, 5 + b % 2, P * h:P * h + P],
                            scalar=key[:, h, NPROMPT + b:NPROMPT + b + 1], in1=st,
                            op0=ALU.mult, op1=ALU.add).then_inc(st_new, 1)
                dve.wait_ge(g_sig, l + 1)
                dve.wait_ge(gelu_sig, l + 1)
                link(dve.tensor_tensor(zg[:, :, :], zg[:, :, :], zf[:, :, :], ALU.mult))
                link(dve.tensor_tensor(zr[:, :, :], zr[:, :, :], cum[:, :, :], ALU.mult))

                dve.wait_ge(decay_ready, 8 * (l + 1))
                dve.wait_ge(st_new, NSAMPLE * HEADS * (l + 1))
                link(dve.tensor_tensor(cum[:, :, :], lev[1][:, :, :], lev[1][:, :, :], ALU.mult))
                dve.scalar_tensor_tensor(out=key[:, :, :], in0=cum[:, :, :], scalar=1.0,
                                         in1=key[:, :, :], op0=ALU.add, op1=ALU.mult
                                         ).then_inc(om_ready, 1)
                link(dve.tensor_tensor(lev[2][:, :, :], lev[2][:, :, :], xc[:, :, :], ALU.mult))
                dve.wait_ge(o_done, l + 1)
                dve.tensor_copy(oT[:, :, :], ps[:, 0:4, 0:T]).then_inc(o_ready, 1)
                dve.wait_ge(om_root, l + 1)
                link(dve.tensor_tensor(lev[2][:, :, :], lev[2][:, :, :], key[:, :, :], ALU.mult))
                for j in range(HEADS):
                    link(dve.tensor_tensor_scan(xc[:, j, 0:NPROMPT], lev[1][:, j, 0:NPROMPT],
                                                lev[2][:, j, 0:NPROMPT], 0.0, ALU.mult, ALU.add))
                h0 = vecT[:, V_SLRU + 32 * l:V_SLRU + 32 * l + 32].rearrange("p (b j) -> p j b",
                                                                            j=HEADS)
                link(dve.tensor_tensor(xcs, h0, lev[1][:, :, NPROMPT:T], ALU.mult))
                link(dve.tensor_tensor(xcs, xcs, lev[2][:, :, NPROMPT:T], ALU.add))
                ls = outs[:, O_LRUS:O_LRUS + 32].rearrange("p (b j) -> p j b", j=HEADS)
                link(dve.tensor_copy(ls, xcs))
                dve.tensor_copy(outs[:, O_LRUP:O_LRUP + 4, None],
                                xc[:, :, NPROMPT - 1:NPROMPT]).then_inc(rows_in, 1)
                dve.wait_ge(rows_in, l + 1)
                link(dve.tensor_tensor(xc[:, :, :], xc[:, :, :], zr[:, :, :], ALU.mult))
                dve.sem_inc(merged, HEADS)
                dve.wait_ge(o_root, l + 1)
                link(dve.reciprocal(zf[:, :, :], zf[:, :, :]))
                link(dve.tensor_tensor(zf[:, :, :], zf[:, :, :], zg[:, :, :], ALU.mult))
                for h in range(HEADS):
                    dve.scalar_tensor_tensor(out=oT[:, h, :], in0=oT[:, h, :],
                                             scalar=v(V_HG + 4 * l + h), in1=zf[:, h, :],
                                             op0=ALU.mult, op1=ALU.mult).then_inc(merged, 1)
                for n, c in enumerate(MERGE_ORDER):
                    dve.wait_ge(m_hi_made, DC * l + n + 1)
                    src = oT[:, c, :] if c < HEADS else xc[:, c - HEADS, :]
                    dve.tensor_tensor(h_lo[:, c, :], src, h_hi[:, c, :].bitcast(F32),
                                      ALU.subtract).then_inc(m_split, 1)
                lo(ob + 3)
                dve.wait_ge(rows_turned, l + 1)
                if l:
                    dve.wait_ge(rows_stored, 16 * (1 + 4 * l))
                dve.tensor_copy(outs_t[0:O_COLS, :], ps[0:O_COLS, 5, 0:P]).then_inc(rows_ready, 1)
                first = 8 if l == 0 else 16 + 8 * FF_STEPS
                for c in range(DC):
                    dve.wait_ge(y_done, (0 if l == 0 else DC + DC * FF_STEPS) + c + 1)
                    dve.tensor_tensor(xT[:, c, :], xT[:, c, :], ps[:, c % 4, 0:T], ALU.add
                                      ).then_inc(x_sum, 1)

            norm(0, V_N1)
            norm_lo(0)
            mixer(0)
            norm(1, V_N2)
            norm_lo(1)
            lo(FF_BASE)
            lo(FF_BASE + 1)

            def ff_gate(s, parity, w3_used):
                dve.wait_ge(used, w3_used)
                dve.wait_ge(ff_silu_done, s + 1)
                dve.wait_ge(ff_split, s)
                dve.tensor_tensor(ff_g[:, :, :], ff_silu[:, :, :], ps[:, 2:4, 0:T], ALU.mult
                                  ).then_inc(ff_g_done, 1)
                dve.wait_ge(ff_hi_done, s + 1)
                dve.tensor_tensor(ff_lo[:, parity, :, :], ff_g[:, :, :],
                                  ff_hi[:, parity, :, :].bitcast(F32), ALU.subtract
                                  ).then_inc(ff_split, 1)

            def ff_add(tiles):
                for c in range(DC):
                    dve.wait_ge(y_done, tiles + (DC + c + 1))
                    dve.wait_ge(x_sum, tiles + (16 + c - 7))
                    dve.tensor_tensor(xT[:, c, :], xT[:, c, :], ps[:, 4 + c % 4, 0:T], ALU.add
                                      ).then_inc(x_sum, 1)

            def ff_step(i, k, add, first=False):
                b = FF_BASE + 2 + 3 * k
                s = i * 2 + (k + 1)
                lo(b, i)
                ff_gate(s - 1, k, i * RAW + (b if first else b - 1))
                if add:
                    ff_add((s - 2) * DC)
                lo(b + 1, i)
                lo(b + 2, i)

            ff_step(0, 0, False, first=True)
            ff_step(0, 1, True)
            with dve.Fori(1, (FF_STEPS - 1) // 2) as i:
                for k in range(2):
                    ff_step(i, k, True)
            ff_gate(FF_STEPS - 1, 0, FF_BASE + 3 * FF_STEPS - 2)
            ff_add((FF_STEPS - 2) * DC)
            lo(FF_BASE + 3 * FF_STEPS - 1)
            ff_add((FF_STEPS - 1) * DC)
            norm(2, V_N1 + 8)
            norm_lo(2)
            mixer(1)
            norm(3, V_N2 + 8)

            L, E1, W, S1, L2, S2, GATE, CHO, DD, EX, POS, R3 = (rt[:, k, :, :] for k in range(12))
            b3 = lambda a: a[:, :, 0:1].broadcast_to([P, 3, EXPERTS])
            dve.wait_ge(st_stored, 16 * DEPTH)
            dve.wait_ge(fin_stored, 16 * DEPTH)
            dve.wait_ge(rows_stored, 16 * (1 + 4 * DEPTH))
            link(dve.memset(h_tok[:, :, 2, :].bitcast(F32), 0.0))
            dve.sem_inc(ht_zero, 1)
            link(dve.memset(rt[:, :, :, :], 0.0))
            dve.wait_ge(logits_done, 1)
            link(dve.tensor_copy(L[:, 0:2, :], ps[:, 0, 0:16].rearrange("p (t e) -> p t e", t=2)))
            link(dve.tensor_copy(L[0:8, 2:3, :], ps[0:8, 0, 16:24].rearrange(
                "p (t e) -> p t e", t=1)))
            rank3 = rank[:, None, :].broadcast_to([P, 3, EXPERTS])

            def first_best(src, sel, best):
                link(dve.tensor_reduce(best[:, :, 0:1], src, AX.X, ALU.max))
                link(dve.tensor_tensor(E1, src, b3(best), ALU.is_equal))
                link(dve.tensor_tensor(W, E1, rank3, ALU.mult))
                link(dve.tensor_reduce(E1[:, :, 0:1], W, AX.X, ALU.max))
                link(dve.tensor_tensor(sel, W, b3(E1), ALU.is_equal))

            first_best(L, S1, GATE)
            link(dve.scalar_tensor_tensor(out=L2, in0=S1, scalar=-3.0e38, in1=L, op0=ALU.mult,
                                          op1=ALU.add))
            first_best(L2, S2, CHO)
            dve.tensor_tensor(DD[:, :, 0:1], CHO[:, :, 0:1], GATE[:, :, 0:1], ALU.subtract
                              ).then_inc(margin_ready, 1)
            dve.wait_ge(margin_exp, 1)
            link(dve.tensor_scalar(DD[:, :, 1:2], EX[:, :, 0:1], 1.0, None, ALU.add))
            link(dve.reciprocal(DD[:, :, 2:3], DD[:, :, 1:2]))
            link(dve.tensor_tensor(DD[:, :, 3:4], DD[:, :, 2:3], EX[:, :, 0:1], ALU.mult))
            link(dve.tensor_tensor(W, S1, DD[:, :, 2:3].broadcast_to([P, 3, EXPERTS]), ALU.mult))
            link(dve.tensor_tensor(E1, S2, DD[:, :, 3:4].broadcast_to([P, 3, EXPERTS]), ALU.mult))
            link(dve.tensor_tensor(GATE, W, E1, ALU.add))
            link(dve.tensor_tensor(W, S1, S2, ALU.add))
            dve.tensor_tensor(CHO, W, valid[:, :, None].broadcast_to([P, 3, EXPERTS]), ALU.mult
                              ).then_inc(chosen_ready, 1)
            dve.wait_ge(chosen_ready, 1)
            link(dve.tensor_scalar(W, CHO, -8192.0, 8192.0, ALU.mult, ALU.add))
            dve.wait_ge(pos_done, 1)
            link(dve.tensor_tensor(place[:, :, 0:EXPERTS], W,
                                   ps[:, 1, 0:24].rearrange("p (t e) -> p t e", t=3), ALU.add))
            link(dve.tensor_scalar(place[:, :, EXPERTS:EXPERTS + 1], place[:, :, 0:1],
                                   -float(SLOTS), None, ALU.add))
            link(dve.tensor_reduce(R3[:, 0, 0:1], ps[:, 1, 24:32], AX.X, ALU.max))
            link(dve.tensor_scalar(R3[:, 0, 1:2], R3[:, 0, 0:1], float(SLOTS) + 0.5, 1.0,
                                   ALU.is_gt, ALU.add))
            link(dve.scalar_tensor_tensor(out=blocks_i[:, 0:1], in0=R3[:, 0, 0:1],
                                          scalar=2.0 * SLOTS + 0.5, in1=R3[:, 0, 1:2],
                                          op0=ALU.is_gt, op1=ALU.add))
            dve.sem_inc(blocks_ready, 1)
            for n in range(6):
                t, half = n // 2, n % 2
                rows = TOKEN_TILES[t][2]
                cols = slice(512 * half, 512 * half + 512)
                dve.wait_ge(ht_hi, n + 1)
                dve.tensor_tensor(h_tok[0:rows, 1, t, cols], ps[0:rows, 2 + half, :],
                                  h_tok[0:rows, 0, t, cols].bitcast(F32), ALU.subtract
                                  ).then_inc(ht_split, 1)

            dve.wait_ge(ht_split, 6)
            link(dve.memset(ps[:, 3:5, :], 0.0))
            link(dve.memset(gslot, 0.0))
            link(dve.memset(pickT[:, :].bitcast(F32), 0.0))
            for count in (added, y_split, g_done, gT_split, pickT_ready):
                dve.sem_inc(count, START)

            def make_pick(it, column):
                dve.wait_ge(pickT_done, START + it)
                for t in range(3):
                    dve.tensor_scalar(pick[:, t, :], iota[:, :],
                                      place[:, t, bass.ds(column, 1)], None, ALU.is_equal
                                      ).then_inc(pick_ready, 1)

            def gather_low(it):
                for half in range(2):
                    dve.wait_ge(gathered, it * 4 + (3 + half))
                    dve.tensor_copy(xg[:, 1, 4 * half:4 * half + 4, :],
                                    ps[:, 5 + half, :].rearrange("p (c n) -> p c n", c=4)
                                    ).then_inc(xg_lo, 1)

            def y_gate(it):
                dve.wait_ge(used, it * EX_UNITS + EX_BASE)
                dve.wait_ge(pickT_ready, START + it * 2)
                dve.wait_ge(y_split, START + it)
                for half in range(2):
                    dve.tensor_scalar(y_f[:, 512 * half:512 * half + 512], ps[:, 3 + half, :],
                                      gslot, None, ALU.mult).then_inc(y_gated, 1)

            def y_low(it):
                dve.wait_ge(y_hi, it + 1)
                dve.tensor_tensor(y_ex[:, 1, :], y_f[:, :], y_ex[:, 0, :].bitcast(F32),
                                  ALU.subtract).then_inc(y_split, 1)

            def add(it, c):
                dve.wait_ge(spread, START + it * DC + (c + 1))
                dve.wait_ge(added, START + it * DC + c)
                dve.tensor_tensor(xT[:, c, :], xT[:, c, :], ps[:, 5 + c % 2, 0:T],
                                  ALU.add).then_inc(added, 1)

            make_pick(0, 0)
            gather_low(0)
            nb = dve.value_load(blocks_i[0:1, 0:1], min_val=1, max_val=3)
            with dve.Fori(0, nb) as b:
                with dve.Fori(0, EXPERTS) as e:
                    it = b * EXPERTS + e
                    s0 = it * EX_STEPS
                    lo(EX_BASE, s0)
                    lo(EX_BASE + 1, s0)
                    y_gate(it)
                    lo(EX_BASE + 2, s0)
                    y_low(it)
                    lo(EX_BASE + 3, s0)

                    def gate(s, w3_used):
                        dve.wait_ge(used, w3_used)
                        dve.wait_ge(silu_done, s + 1)
                        dve.wait_ge(g_turned, START + s)
                        dve.tensor_tensor(ex_g[:, :], ex_silu[:, :], ps[:, 1, :], ALU.mult
                                          ).then_inc(g_done, 1)

                    def turned_low(s):
                        dve.wait_ge(gT_hi, s + 1)
                        dve.tensor_tensor(gT[:, 1, :, :].rearrange("p j n -> p (j n)"),
                                          ps[:, 2, :],
                                          gT[:, 0, :, :].rearrange("p j n -> p (j n)").bitcast(
                                              F32), ALU.subtract).then_inc(gT_split, 1)

                    def step(i, w3_used, spreading=False):
                        lo(EX_BASE + 4, i)
                        gate(i, i * RAW + w3_used)
                        for j in range(1, 4):
                            lo(EX_BASE + 4 + j, i)
                            if spreading:
                                add(it, 2 * j - 2)
                                add(it, 2 * j - 1)
                        turned_low(i)
                        lo(EX_BASE + 8, i)
                        if spreading:
                            add(it, DC - 2)
                            add(it, DC - 1)
                            dve.wait_ge(pickT_done, START + it + 1)
                            dve.tensor_copy(pickT[:, :], ps[:, 7, 0:T]).then_inc(pickT_ready, 1)
                            dve.tensor_copy(gslot, ps[:, 7, T:T + 1]).then_inc(pickT_ready, 1)
                        lo(EX_BASE + 9, i)

                    step(s0, EX_BASE + 4, spreading=True)
                    make_pick(it + 1, e + 1)
                    with dve.Fori(2, EX_STEPS) as s:
                        step(s0 + (s - 1), EX_BASE + 2)
                    lo(EX_BASE + EX_UNITS - 2, s0)
                    lo(EX_BASE + EX_UNITS - 1, s0)
                    gate(s0 + (EX_STEPS - 1), s0 * RAW + (EX_BASE + EX_UNITS - 4))
                    turned_low(s0 + (EX_STEPS - 1))
                    gather_low(it + 1)
                dve.wait_ge(pick_ready, (b * EXPERTS + EXPERTS) * 3 + 3)
                dve.tensor_scalar(place[:, :, :], place[:, :, :], -float(SLOTS), None, ALU.add
                                  ).then_inc(pos_moved, 1)
                dve.wait_ge(pos_moved, b + 1)
            y_gate(nb * EXPERTS)
            y_low(nb * EXPERTS)
            for c in range(DC):
                add(nb * EXPERTS, c)
            dve.wait_ge(added, START + nb * (EXPERTS * DC) + DC)
            dve.sem_inc(x_sum, 1)
            norm(4, V_NF)
            for n in range(6):
                t, half = n // 2, n % 2
                rows = TOKEN_TILES[t][2]
                dve.wait_ge(yt_turned, n + 1)
                dve.tensor_copy(y_rows[0:rows, t, 512 * half:512 * half + 512],
                                ps[0:rows, half, :]).then_inc(yt_ready, 1)

        @block.tensor
        def _(pe):
            def mm3(out, l_hi, l_lo, r_hi, r_lo, start, stop):
                pe.matmul(out, l_hi, r_hi, start=start, stop=False)
                pe.matmul(out, l_hi, r_lo, start=False, stop=False)
                return pe.matmul(out, l_lo, r_hi, start=False, stop=stop)

            pe.wait_ge(consts, 1)
            pe.wait_ge(x_landed, 32)
            for c in range(DC):
                if c >= 4:
                    pe.wait_ge(x_sum, c - 3)
                for t, t0, n in TOKEN_TILES:
                    ins = pe.transpose(ps[:, c % 4, t0:t0 + n],
                                       x_rows[0:n, t, c * P:(c + 1) * P], ident[0:n, 0:n])
                ins.then_inc(x_turned, 1)
            pe.wait_ge(vec_landed, 16 * 13)
            for k, (col, n) in enumerate(((0, V_ROWS), (V_SLRU, 64), (V_SCONV, 96),
                                          (V_SCONV + 96, 96))):
                ins = pe.transpose(ps[:, 5, col:col + n], vec_rows[0:n, k, :], ident[0:n, 0:n])
            ins.then_inc(vec_turned, 1)

            def norm(n):
                for c in range(DC):
                    pe.wait_ge(sq_ready, DC * n + c + 1)
                    ins = pe.matmul(ps[:, NORM_BANK[n], 0:T], ones[:, :], sq[:, c, :], start=(c == 0),
                                    stop=(c == DC - 1))
                ins.then_inc(ssq_done, 1)

            def project(base, i, tile0, j, bank):
                _, s, _, _ = unit_of(base)
                wh = w_hi[:, s, :].rearrange("p (c n) -> p c n", c=DC)
                wl = w_lo[:, s, :].rearrange("p (c n) -> p c n", c=DC)
                cols = slice(P * j, P * j + P)
                for c in range(DC):
                    ins = mm3(ps[:, bank, 0:T], wh[:, c, cols], wl[:, c, cols], h_hi[:, c, :],
                              h_lo[:, c, :], c == 0, c == DC - 1)
                return ins

            def mixer(l, norm_n):
                ib, ob = IN_BASE[l], OUT_BASE[l]
                pe.wait_ge(h_split, DC * norm_n + DC)
                with pe.Fori(0, IN_UNITS // RAW) as i:
                    for u in range(RAW):
                        pe.wait_ge(split, i * RAW + (ib + u + 1))
                        for j in range(2):
                            n = 2 * u + j
                            pe.wait_ge(z_free, i * 12 + (24 * l + n + 1))
                            ins = project(ib + u, 0, 0, j, n % 4)
                            ins.then_inc(z_done, 1)
                        pe.wait_ge(z_done, i * 12 + (24 * l + n + 1))
                        pe.sem_inc(used, 1)
                pe.wait_ge(z_free, 4 + 24 * l + 24)
                for c in range(2):
                    for h in range(HEADS):
                        ins = pe.transpose(ps[:, 6 + c, P * h:P * h + P],
                                           zv[:, h, P * c:P * c + P], ident[:, :])
                ins.then_inc(v_turned, 1)
                n = 0

                def scores(left, right, c, across=False):
                    nonlocal n
                    if n >= 4:
                        pe.wait_ge(sc_taken, PRODUCTS * l + n - 3)
                    for h in range(HEADS):
                        rc = 1 if across else c
                        ins = pe.matmul(ps[:, n % 4, P * h:P * h + P],
                                        left[:, h, P * c:P * c + P],
                                        right[:, h, P * rc:P * rc + P], start=True, stop=True)
                    ins.then_inc(sc_done, 1)
                    n += 1

                pe.wait_ge(q_ready, l + 1)
                scores(key, zq, 0)
                scores(key, zq, 1)
                for k in range(7):
                    pe.wait_ge(lev_ready, 16 * l + 2 * k + 2)
                    scores(lev[k % 3], lev[k % 3], 0)
                    scores(lev[k % 3], lev[k % 3], 1)
                pe.wait_ge(lev_ready, 16 * (l + 1))
                scores(lev[7 % 3], lev[7 % 3], 0, across=True)
                pe.wait_ge(v_ready, l + 1)
                pe.wait_ge(kd_ready, l + 1)
                for c in range(2):
                    for h in range(HEADS):
                        ins = pe.transpose(ps[:, 6 + c, P * h:P * h + P],
                                           lev[2][:, h, P * c:P * c + P], ident[:, :])
                ins.then_inc(kd_turned, 1)
                pe.wait_ge(sc_taken, PRODUCTS * (l + 1))
                for h in range(HEADS):
                    pe.matmul(ps[:, h, 0:P], v_tok[:, 0, h, :], sc[:, 0, h, :], start=True,
                              stop=True)
                    pe.matmul(ps[:, h, P:2 * P], v_tok[:, 0, h, :], sc[:, 2, h, :], start=True,
                              stop=False)
                    pe.matmul(ps[:, h, P:2 * P], v_tok[:, 1, h, :], sc[:, 1, h, :], start=False,
                              stop=True)
                pe.wait_ge(kd_tok_ready, l + 1)
                for h in range(HEADS):
                    for c in range(2):
                        ins = pe.matmul(ps[:, 4, P * h:P * h + P], k_tok[:, c, h, :],
                                        v_tok[:, c, h, :], start=(c == 0), stop=(c == 1))
                ins.then_inc(fin_done, 1)
                for b in range(NSAMPLE + 1):
                    if b < NSAMPLE:
                        pe.wait_ge(diag_ready, NSAMPLE * l + b + 1)
                        if b >= 2:
                            pe.wait_ge(st_new, HEADS * (NSAMPLE * l + b - 1))
                        pe.matmul(ps[:, 5 + b % 2, :], ones[:, :],
                                  v_diag[:, b % 2, :, :].rearrange("p h v -> p (h v)"),
                                  start=True, stop=True).then_inc(kv_done, 1)
                    if b >= 1:
                        pe.wait_ge(st_new, HEADS * (NSAMPLE * l + b))
                        for h in range(HEADS):
                            col = NPROMPT + b - 1
                            ins = pe.matmul(ps[:, h, col:col + 1],
                                            hstate[:, HEADS * (b - 1) + h, :],
                                            zq[:, h, col:col + 1], start=True, stop=True)
                ins.then_inc(o_done, 1)
                pe.wait_ge(conv_ready, l + 1)
                pe.wait_ge(gw_landed, 16 * 8)
                pe.wait_ge(fin_ready, l + 1)
                for n8 in range(8):
                    j = n8 % 4
                    if n8 >= 4:
                        pe.wait_ge(gates_ready, 8 * l + n8 - 3)
                    pe.matmul(ps[:, 4 + j, 0:T], gate_w[:, l, n8 // 4, j, :], lev[0][:, j, :],
                              start=True, stop=True).then_inc(gates_done, 1)
                pe.wait_ge(gates_ready, 8 * (l + 1))
                pe.wait_ge(o_sq, l + 1)
                for h in range(HEADS):
                    ins = pe.matmul(ps[:, 4 + h, 0:T], ones[:, :], zf[:, h, :], start=True,
                                    stop=True)
                ins.then_inc(o_ssq, 1)
                pe.wait_ge(o_root, l + 1)
                pe.wait_ge(rows_in, l + 1)
                pe.transpose(ps[0:O_COLS, 5, 0:P], outs[:, :], ident[:, :]
                             ).then_inc(rows_turned, 1)
                pe.wait_ge(m_split, DC * (l + 1))
                n0 = 0 if l == 0 else DC + DC * FF_STEPS
                xs = 8 if l == 0 else 16 + 8 * FF_STEPS
                for u in range(OUT_UNITS):
                    pe.wait_ge(split, ob + u + 1)
                    for j in range(2):
                        c = 2 * u + j
                        if c >= 4:
                            pe.wait_ge(x_sum, xs + c - 3)
                        project(ob + u, 0, 0, j, c % 4).then_inc(y_done, 1)
                    pe.wait_ge(y_done, n0 + c + 1)
                    pe.sem_inc(used, 1)

            norm(0)
            mixer(0, 0)
            norm(1)
            pe.wait_ge(h_split, 2 * DC)

            def up(base, i, bank):
                pe.wait_ge(split, i * RAW + (base + 1))
                for j in range(2):
                    ins = project(base, 0, 0, j, bank + j)
                ins.then_inc(used, 1)

            def down(base, i, parity, s):
                _, sl, _, _ = unit_of(base)
                wh = w_hi[:, sl, :].rearrange("p (j n) -> p j n", j=2)
                wl = w_lo[:, sl, :].rearrange("p (j n) -> p j n", j=2)
                pe.wait_ge(split, i * RAW + (base + 1))
                pe.wait_ge(ff_split, s + 1)
                for c in range(DC):
                    pe.wait_ge(x_sum, s * DC + (16 + c - 3))
                    for j in range(2):
                        ins = mm3(ps[:, 4 + c % 4, 0:T], wh[:, j, c * P:(c + 1) * P],
                                  wl[:, j, c * P:(c + 1) * P], ff_hi[:, parity, j, :],
                                  ff_lo[:, parity, j, :], j == 0, j == 1)
                    ins.then_inc(y_done, 1)
                pe.wait_ge(y_done, s * DC + 2 * DC)
                pe.sem_inc(used, 1)

            up(FF_BASE, 0, 0)
            up(FF_BASE + 1, 0, 2)
            with pe.Fori(0, (FF_STEPS - 1) // 2) as i:
                for k in range(2):
                    s = i * 2 + (k + 1)
                    b = FF_BASE + 2 + 3 * k
                    pe.wait_ge(ff_silu_done, s)
                    up(b, i, 0)
                    pe.wait_ge(ff_g_done, s)
                    up(b + 1, i, 2)
                    down(b + 2, i, k, s - 1)
            down(FF_BASE + 3 * FF_STEPS - 1, 0, 0, FF_STEPS - 1)
            norm(2)
            mixer(1, 2)
            norm(3)

            pe.wait_ge(rw_landed, 16)
            pe.wait_ge(h_full, 4 * DC)
            for t, t0, n in TOKEN_TILES:
                for c in range(DC):
                    ins = pe.matmul(ps[0:n, 0, 8 * t:8 * t + 8], hF[:, c, t0:t0 + n],
                                    rw[:, c, :], start=(c == 0), stop=(c == DC - 1))
            ins.then_inc(logits_done, 1)

            def turn_tokens(n):
                t, half = n // 2, n % 2
                _, t0, rows = TOKEN_TILES[t]
                if n >= 2:
                    pe.wait_ge(ht_split, n - 1)
                for c in range(4):
                    ins = pe.transpose(ps[0:rows, 2 + half, P * c:P * c + P],
                                       hF[:, 4 * half + c, t0:t0 + rows], ident[:, :])
                ins.then_inc(ht_turned, 1)

            turn_tokens(0)
            turn_tokens(1)
            pe.wait_ge(chosen_ready, 1)
            cho = rt[:, 7, :, :]
            for t in range(3):
                for t2 in range(t + 1):
                    pe.matmul(ps[:, 1, 8 * t:8 * t + 8], (before if t2 == t else ones)[:, :],
                              cho[:, t2, :], start=(t2 == 0), stop=(t2 == t))
            for t in range(3):
                ins = pe.matmul(ps[:, 1, 24:32], ones[:, :], cho[:, t, :], start=(t == 0),
                                stop=(t == 2))
            ins.then_inc(pos_done, 1)
            for n in range(2, 6):
                turn_tokens(n)
            pe.wait_ge(ht_split, 6)
            pe.wait_ge(blocks_ready, 1)
            for count in (spread, g_turned, pickT_done):
                pe.sem_inc(count, START)

            def gather(it, part):
                pe.wait_ge(pick_ready, it * 3 + 3)
                for half in range(2):
                    if part:
                        pe.wait_ge(xg_hi, it * 2 + (half + 1))
                    for c in range(4):
                        for t in range(3):
                            ins = pe.matmul(ps[:, 5 + half, P * c:P * c + P],
                                            h_tok[:, part, t, (4 * half + c) * P:
                                                  (4 * half + c + 1) * P],
                                            pick[:, t, :], start=(t == 0), stop=(t == 2))
                    ins.then_inc(gathered, 1)

            def scatter(it, c):
                if c == 0:
                    pe.wait_ge(pickT_ready, START + it * 2)
                    pe.wait_ge(y_split, START + it + 1)
                    pe.wait_ge(xg_lo, it * 2 + 2)
                if c >= 2:
                    pe.wait_ge(added, START + it * DC + (c - 1))
                pe.matmul(ps[:, 5 + c % 2, 0:T], y_ex[:, 0, c * P:(c + 1) * P],
                          pickT[:, :], start=True, stop=False)
                pe.matmul(ps[:, 5 + c % 2, 0:T], y_ex[:, 1, c * P:(c + 1) * P],
                          pickT[:, :], start=False, stop=True).then_inc(spread, 1)

            gather(0, 0)
            gather(0, 1)
            nb = pe.value_load(blocks_i[0:1, 0:1], min_val=1, max_val=3)
            with pe.Fori(0, nb) as b:
                with pe.Fori(0, EXPERTS) as e:
                    it = b * EXPERTS + e
                    s0 = it * EX_STEPS

                    def up_half(base, i, bank, half):
                        _, sl, _, _ = unit_of(base)
                        wh = w_hi[:, sl, :].rearrange("p (c n) -> p c n", c=4)
                        wl = w_lo[:, sl, :].rearrange("p (c n) -> p c n", c=4)
                        pe.wait_ge(split, i * RAW + (base + 1))
                        for c in range(4):
                            k = 4 * half + c
                            ins = mm3(ps[:, bank, :], xg[:, 0, k, :], xg[:, 1, k, :],
                                      wh[:, c, :], wl[:, c, :], k == 0, k == DC - 1)
                        ins.then_inc(used, 1)

                    def turn(s):
                        pe.wait_ge(g_done, START + s + 1)
                        pe.wait_ge(gT_split, START + s)
                        for j in range(4):
                            ins = pe.transpose(ps[:, 2, P * j:P * j + P],
                                               ex_g[:, P * j:P * j + P], ident[:, :])
                        ins.then_inc(g_turned, 1)

                    def down_half(base, i, s, half, first, last):
                        _, sl, _, _ = unit_of(base)
                        wh = w_hi[:, sl, :].rearrange("p (j n) -> p j n", j=2)
                        wl = w_lo[:, sl, :].rearrange("p (j n) -> p j n", j=2)
                        pe.wait_ge(split, i * RAW + (base + 1))
                        if half == 0:
                            pe.wait_ge(gT_split, START + s + 1)
                        for j in range(2):
                            k = 2 * half + j
                            for n in range(2):
                                ins = mm3(ps[:, 3 + n, :], gT[:, 0, k, :], gT[:, 1, k, :],
                                          wh[:, j, 512 * n:512 * n + 512],
                                          wl[:, j, 512 * n:512 * n + 512],
                                          first and k == 0, last and k == 3)
                        ins.then_inc(used, 1)

                    def step(i, s, first):
                        b0 = EX_BASE + 4
                        pe.wait_ge(silu_done, s + 1)
                        up_half(b0, i, 0, 0)
                        if first:
                            scatter(it, 0)
                            scatter(it, 1)
                        up_half(b0 + 1, i, 0, 1)
                        turn(s)
                        if first:
                            scatter(it, 2)
                            scatter(it, 3)
                        up_half(b0 + 2, i, 1, 0)
                        if first:
                            scatter(it, 4)
                            scatter(it, 5)
                        up_half(b0 + 3, i, 1, 1)
                        if first:
                            scatter(it, 6)
                            scatter(it, 7)
                            for t, t0, n in TOKEN_TILES:
                                pe.transpose(ps[:, 7, t0:t0 + n], pick[0:n, t, :].bitcast(F32),
                                             ident[0:n, 0:n])
                            for t in range(3):
                                ins = pe.matmul(ps[:, 7, T:T + 1], pick[:, t, :].bitcast(F32),
                                                rt[:, 6, t, bass.ds(e, 1)], start=(t == 0),
                                                stop=(t == 2))
                            ins.then_inc(pickT_done, 1)
                        down_half(b0 + 4, i, s, 0, first, False)
                        down_half(b0 + 5, i, s, 1, False, False)

                    pe.wait_ge(xg_hi, it * 2 + 2)
                    pe.wait_ge(xg_lo, it * 2 + 2)
                    up_half(EX_BASE, s0, 0, 0)
                    up_half(EX_BASE + 1, s0, 0, 1)
                    up_half(EX_BASE + 2, s0, 1, 0)
                    up_half(EX_BASE + 3, s0, 1, 1)
                    pe.wait_ge(y_gated, it * 2 + 2)
                    step(s0, s0, True)
                    with pe.Fori(2, EX_STEPS) as s:
                        step(s0 + (s - 1), s0 + (s - 1), False)
                    pe.wait_ge(added, START + it * DC + DC)
                    gather(it + 1, 0)
                    turn(s0 + (EX_STEPS - 1))
                    gather(it + 1, 1)
                    down_half(EX_BASE + EX_UNITS - 2, s0, s0 + (EX_STEPS - 1), 0, False, False)
                    down_half(EX_BASE + EX_UNITS - 1, s0, s0 + (EX_STEPS - 1), 1, False, True)
            for c in range(DC):
                scatter(nb * EXPERTS, c)
            norm(4)
            pe.wait_ge(h_full, 5 * DC)
            for n in range(6):
                t, half = n // 2, n % 2
                _, t0, rows = TOKEN_TILES[t]
                if n >= 2:
                    pe.wait_ge(yt_ready, n - 1)
                for c in range(4):
                    ins = pe.transpose(ps[0:rows, half, P * c:P * c + P],
                                       hF[:, 4 * half + c, t0:t0 + rows], ident[:, :])
                ins.then_inc(yt_turned, 1)


_INS = ['x_prompt', 'x_sample', 'state_hgrn', 'state_lru', 'state_conv', 'norm1_g', 'w_in',
        'lower_bounds', 'hg_norm_g', 'conv_w', 'conv_b', 'w_ra', 'b_ra', 'w_ix', 'b_ix',
        'lru_lambda', 'w_out', 'norm2_g', 'ffn_w1', 'ffn_w3', 'ffn_w2', 'router_w', 'moe_w1',
        'moe_w3', 'moe_w2', 'final_norm_g']
_OUTS = [(1, 256, 1024), (8, 1, 1024), (2, 1, 4, 128, 128), (2, 1, 512), (2, 1, 3, 512),
         (2, 8, 4, 128, 128), (2, 8, 512), (2, 8, 3, 512)]


def kernel(**inputs):
    import numpy as _np
    import concourse.bacc as _bacc
    from concourse import mybir as _mybir
    from concourse.bass_utils import run_bass_kernel_spmd as _run

    nc = _bacc.Bacc("TRN2", target_bir_lowering=False, num_devices=1)
    arrays, args = {}, []
    for name in _INS:
        a = _np.ascontiguousarray(inputs[name])
        arrays[f"in_{name}_dram"] = a
        args.append(nc.dram_tensor(f"in_{name}_dram", a.shape, _mybir.dt.from_np(a.dtype),
                                   kind="ExternalInput").ap())
    for i, shape in enumerate(_OUTS):
        args.append(nc.dram_tensor(f"out_{i}_dram", shape, _mybir.dt.float32,
                                   kind="ExternalOutput").ap())
    trunk(nc, *args)
    r = _run(nc, [arrays], core_ids=[0])
    return tuple(r.results[0][f"out_{i}_dram"] for i in range(len(_OUTS)))
```

```python
import concourse.bass as bass
from concourse import mybir
from contextlib import ExitStack

F32 = mybir.dt.float32
F32R = mybir.dt.float32r
I32 = mybir.dt.int32
ALU = mybir.AluOpType
ACT = mybir.ActivationFunctionType
AX = mybir.AxisListType

D, P = 1024, 128
DC = D // P
DEPTH = 2
NPROMPT, NSAMPLE = 256, 8
T = NPROMPT + NSAMPLE
HEADS = 4
TAPS = 4
D_FF, D_FFE, EXPERTS = 2816, 3584, 8
EPS = 1e-6
MERGE_ORDER = [4, 5, 6, 7, 0, 1, 2, 3]
SLOTS = P
PRODUCTS = 17
START = 1
GATE_BANK = [2, 3, 5]
TURN_BANK = [2, 3, 4, 7]
LOGIT_BANK = [0, 5, 6]
STATES_FIRST = 2
NORM_BANK = [4, 4, 0, 4, 4]
TINY, LN_TINY = 1e-19, -43.74911676688687

TOKEN_TILES = [(0, 0, 128), (1, 128, 128), (2, 256, 8)]

RAW, SPLIT = 6, 3
EARLY = [1, 2]
LEVEL_LAG = SPLIT + 4
UNIT = 2048
IN_UNITS, OUT_UNITS = 12, 4
FF_STEPS = D_FF // 256
EX_STEPS = D_FFE // 512
IN_BASE = [0, IN_UNITS + OUT_UNITS + 3 * FF_STEPS]
OUT_BASE = [b + IN_UNITS for b in IN_BASE]
FF_BASE = OUT_BASE[0] + OUT_UNITS
EX_BASE = OUT_BASE[1] + OUT_UNITS
EX_UNITS = 6 * EX_STEPS
IN_COLS = [512, 0, 1024, 2048, 2560, 1536]

V_N1, V_N2, V_NF, V_LB, V_HG, V_CW, V_CB, V_RA, V_IX, V_LAM, V_ROWS = (
    0, 16, 32, 40, 48, 56, 88, 96, 104, 112, 120)
V_SLRU, V_SCONV, V_COLS = 128, 192, 384

O_LRUP, O_CONVP, O_LRUS, O_XRS, O_COLS = 0, 4, 16, 48, 80


def trunk(nc, x_prompt, x_sample, state_hgrn, state_lru, state_conv, norm1_g, w_in, lower_bounds,
          hg_norm_g, conv_w, conv_b, w_ra, b_ra, w_ix, b_ix, lru_lambda, w_out, norm2_g,
          ffn_w1, ffn_w3, ffn_w2, router_w, moe_w1, moe_w3, moe_w2, final_norm_g,
          y_prompt, y_sample, hgrn_prompt, lru_prompt, conv_prompt,
          hgrn_sample, lru_sample, conv_sample):
    ctx = ExitStack()
    with ctx:
        base0 = (nc.sbuf_base + 31) // 32 * 32
        slab_bytes = (nc.sbuf_usable_end - base0 - 64) // 32 * 32
        ctx.enter_context(nc.sbuf_tensor("slab", [P, slab_bytes // 4], F32))
        places = {}

        def at(name, offset, shape, dt=F32):
            size = 4
            for n in shape:
                size *= n
            assert offset % 32 == 0 and offset + size <= slab_bytes, (name, offset, size)
            places[name] = offset + (size + 31) // 32 * 32
            return nc.alloc_sbuf_tensor_at(name, [P] + list(shape), dt, offset=base0 + offset)

        def end(name):
            return places[name]

        raw = at("raw", 0, [RAW, UNIT])
        w_hi = at("w_hi", end("raw"), [SPLIT, UNIT], F32R)
        w_lo = at("w_lo", end("w_hi"), [SPLIT, UNIT], F32R)
        xT = at("xT", end("w_lo"), [DC, T])
        ident = at("ident", end("xT"), [P])
        ones_r = at("ones", end("ident"), [P], F32R)
        ones = ones_r[:, :].bitcast(F32)
        iota = at("iota", end("ones"), [P])
        before = at("before", end("iota"), [P])
        masks = at("masks", end("before"), [7, P], I32)
        vecT = at("vecT", end("masks"), [V_COLS])
        gate_w = at("gate_w", end("vecT"), [DEPTH, 2, HEADS, P])
        rw = at("rw", end("gate_w"), [DC, EXPERTS])
        small = at("small", end("rw"), [160])
        HH = end("small")
        h_hi = at("h_hi", HH, [DC, T], F32R)
        h_lo = at("h_lo", end("h_hi"), [DC, T], F32R)
        hstate = at("hstate", HH, [NSAMPLE * HEADS, P])
        WORK = end("h_lo")
        zq = at("zq", WORK, [HEADS, T])
        zf = at("zf", end("zq"), [HEADS, T])
        zv = at("zv", end("zf"), [HEADS, T])
        zg = at("zg", end("zv"), [HEADS, T])
        zx = at("zx", end("zg"), [HEADS, T])
        zr = at("zr", end("zx"), [HEADS, T])
        forget = at("forget", end("zr"), [HEADS, T])
        key = at("key", end("forget"), [HEADS, T])
        cum = at("cum", end("key"), [HEADS, T])
        lev = [at("lev0", end("cum"), [HEADS, T])]
        lev.append(at("lev1", end("lev0"), [HEADS, T]))
        lev.append(at("lev2", end("lev1"), [HEADS, T]))
        sc = at("sc", end("lev2"), [3, HEADS, P])
        v_tok = at("v_tok", end("sc"), [2, HEADS, P])
        k_tok = at("k_tok", end("v_tok"), [2, HEADS, P])
        v_diag = [at("v_diag0", end("v_tok"), [2, HEADS, P], F32R),
                  at("v_diag1", end("key"), [2, HEADS, P], F32R)]
        xc = at("xc", end("k_tok"), [HEADS, T])
        heads = lev[0]
        m_hi = at("m_hi", places["lev0"], [DC, T], F32R)
        m_lo = at("m_lo", places["lev2"], [DC, T], F32R)
        s_fin = at("s_fin", end("xc"), [HEADS, P])
        outs = at("outs", end("s_fin"), [O_COLS])
        outs_t = at("outs_t", end("outs"), [P])
        vs = at("vs", end("outs_t"), [2, HEADS, NSAMPLE], F32R)
        vec_rows = at("vec_rows", end("lev2"), [4, P])
        xor_st = at("xor_st", end("vec_rows"), [4, P], I32)
        xor_f = at("xor_f", end("xor_st"), [2, P])
        sq = at("sq", WORK, [DC, T])
        hF = at("hF", end("sq"), [DC, T])
        rstd = at("rstd", end("hF"), [2, T])
        x_rows = at("x_rows", end("rstd"), [3, D])
        ff_silu = at("ff_silu", end("rstd"), [2, T])
        ff_g = at("ff_g", end("ff_silu"), [2, T])
        ff_hi = at("ff_hi", end("ff_g"), [2, 2, T], F32R)
        ff_lo = at("ff_lo", end("ff_hi"), [2, 2, T], F32R)
        h_tok = at("h_tok", end("hF"), [2, 3, D], F32R)
        xg = at("xg", end("h_tok"), [2, DC, P], F32R)
        pick = at("pick", end("xg"), [3, P], F32R)
        pickT = at("pickT", end("pick"), [T], F32R)
        ex_silu = at("ex_silu", end("pickT"), [512])
        ex_g = at("ex_g", end("ex_silu"), [512])
        gT = at("gT", end("ex_g"), [2, 4, P], F32R)
        y_ex = at("y_ex", end("gT"), [2, D], F32R)
        y_f = at("y_f", end("y_ex"), [D])
        rt = at("rt", HH, [16, 3, EXPERTS])
        blocks_i = at("blocks_i", end("rt"), [8], I32)
        place = at("place", end("blocks_i"), [3, EXPERTS + 1])
        y_rows = at("y_rows", end("hF"), [3, D])

        ps = ctx.enter_context(nc.psum_tensor("ps", [P, 8, 512], F32))

        eps = small[:, 0:1]
        lbv = small[:, 1:9]
        omlb = small[:, 9:17]
        crate = small[:, 17:25]
        ncrate = small[:, 25:33]
        rank = small[:, 33:41]
        valid = small[:, 41:44]
        gslot = small[:, 44:45]
        unused = small[:, 45:46]
        tmp = small[:, 48:160]

        names = {}

        def sem(name):
            names[name] = ctx.enter_context(nc.semaphore(name))
            return names[name]

        landed = [sem(f"landed{i}") for i in range(RAW)]
        hi_made = sem("hi_made")
        split = sem("split")
        used = sem("used")
        x_landed, vec_landed, gw_landed = sem("x_landed"), sem("vec_landed"), sem("gw_landed")
        rw_landed = sem("rw_landed")
        consts = sem("consts")
        pool_step, dve_step, act_step = sem("pool_step"), sem("dve_step"), sem("act_step")
        x_turned, vec_turned, vec_ready = sem("x_turned"), sem("vec_turned"), sem("vec_ready")
        x_sum = sem("x_sum")
        sq_ready, ssq_done, root_done = sem("sq_ready"), sem("ssq_done"), sem("root_done")
        h_full, h_hi_made, h_split = sem("h_full"), sem("h_hi_made"), sem("h_split")
        z_done, z_free = sem("z_done"), sem("z_free")
        f_sig, q_sig, g_sig, gelu_in, gelu_sig = (sem("f_sig"), sem("q_sig"), sem("g_sig"),
                                                  sem("gelu_in"), sem("gelu_sig"))
        f_ready, q_ready, cum_ready = sem("f_ready"), sem("q_ready"), sem("cum_ready")
        gelu_ready, vs_high, vs_split = sem("gelu_ready"), sem("vs_high"), sem("vs_split")
        qf_ready, qk_done, st_read = sem("qf_ready"), sem("qk_done"), sem("st_read")
        clamp_ready, ln_ready = sem("clamp_ready"), sem("ln_ready")
        lev_in, lev_exp, lev_ready = sem("lev_in"), sem("lev_exp"), sem("lev_ready")
        sc_done, sc_taken = sem("sc_done"), sem("sc_taken")
        v_turned, v_ready = sem("v_turned"), sem("v_ready")
        kd_in, kd_exp, kd_ready, kd_turned, kd_tok_ready = (
            sem("kd_in"), sem("kd_exp"), sem("kd_ready"), sem("kd_turned"), sem("kd_tok_ready"))
        fin_done, fin_ready, fin_stored = sem("fin_done"), sem("fin_ready"), sem("fin_stored")
        st_landed, st_decayed, diag_ready = sem("st_landed"), sem("st_decayed"), sem("diag_ready")
        kv_done, st_new, st_stored = sem("kv_done"), sem("st_new"), sem("st_stored")
        o_done, o_ready, o_sq, o_ssq, o_root = (sem("o_done"), sem("o_ready"), sem("o_sq"),
                                                sem("o_ssq"), sem("o_root"))
        conv_ready, gates_done, gates_ready = (sem("conv_ready"), sem("gates_done"),
                                               sem("gates_ready"))
        decay_ready, om_ready, om_root = sem("decay_ready"), sem("om_ready"), sem("om_root")
        merged, m_hi_made, m_split = sem("merged"), sem("m_hi_made"), sem("m_split")
        rows_in, rows_turned, rows_ready, rows_stored = (sem("rows_in"), sem("rows_turned"),
                                                         sem("rows_ready"), sem("rows_stored"))
        setup_in, setup_exp, pos_moved = sem("setup_in"), sem("setup_exp"), sem("pos_moved")
        ff_silu_done, ff_g_done, ff_hi_done, ff_split = (sem("ff_silu_done"), sem("ff_g_done"),
                                                         sem("ff_hi_done"), sem("ff_split"))
        y_done = sem("y_done")
        logits_done, margin_ready, margin_exp = (sem("logits_done"), sem("margin_ready"),
                                                 sem("margin_exp"))
        gates_known = sem("gates_known")
        chosen_ready, pos_done, blocks_ready = (sem("chosen_ready"), sem("pos_done"),
                                                sem("blocks_ready"))
        ht_zero, ht_turned, ht_hi, ht_split = (sem("ht_zero"), sem("ht_turned"), sem("ht_hi"),
                                               sem("ht_split"))
        pick_ready, gathered, xg_hi, xg_lo = (sem("pick_ready"), sem("gathered"), sem("xg_hi"),
                                              sem("xg_lo"))
        pickT_done, pickT_ready = sem("pickT_done"), sem("pickT_ready")
        silu_done, g_done, g_turned, gT_hi, gT_split = (sem("silu_done"), sem("g_done"),
                                                        sem("g_turned"), sem("gT_hi"),
                                                        sem("gT_split"))
        y_gated, y_hi, y_split, spread, added = (sem("y_gated"), sem("y_hi"), sem("y_split"),
                                                 sem("spread"), sem("added"))
        yt_turned, yt_ready, stored = sem("yt_turned"), sem("yt_ready"), sem("stored")

        def unit_of(base, i=0):
            return base % RAW, base % SPLIT, 16 * (base // RAW + 1) + 16 * i, base + RAW * i

        block = ctx.enter_context(nc.Block())

        @block.sync
        def _(sp):
            def load(base, src, i=0, first=False):
                slot, _, _, u = unit_of(base, i)
                if not first:
                    sp.wait_ge(split, u - RAW + 1)
                shape = list(src.shape)
                dst = raw[:, slot, :].rearrange("p (c n) -> p c n", c=shape[1])
                sp.dma_start(dst, src).then_inc(landed[slot], 16)

            sp.dma_start(x_rows[:, 0:2, :], x_prompt.rearrange("a (t p) d -> p (a t) d", p=P)
                         ).then_inc(x_landed, 16)
            sp.dma_start(x_rows[0:NSAMPLE, 2, :], x_sample.rearrange("b s d -> (b s) d")
                         ).then_inc(x_landed, 16)

            def columns(w, n0, n=256):
                return w.rearrange("(c p) n -> p c n", p=P)[:, :, n0:n0 + n]

            def load_in(l):
                for u in range(IN_UNITS):
                    load(IN_BASE[l] + u, columns(w_in[l], IN_COLS[u // 2] + 256 * (u % 2)),
                         first=IN_BASE[l] + u < RAW)
                for u in range(OUT_UNITS):
                    load(OUT_BASE[l] + u, columns(w_out[l], 256 * u))

            sp.wait_ge(vec_landed, 16 * 13)
            load_in(0)
            load(FF_BASE, columns(ffn_w1[0], 0))
            load(FF_BASE + 1, columns(ffn_w3[0], 0))
            with sp.Fori(0, (FF_STEPS - 1) // 2) as i:
                for k in range(2):
                    n0 = i * 512 + 256 * (k + 1)
                    r0 = i * 512 + 256 * k
                    w1c = ffn_w1[0].rearrange("(c p) n -> p c n", p=P)
                    w3c = ffn_w3[0].rearrange("(c p) n -> p c n", p=P)
                    w2r = ffn_w2[0].rearrange("(j p) n -> p j n", p=P)
                    load(FF_BASE + 2 + 3 * k, w1c[:, :, bass.ds(n0, 256)], i)
                    load(FF_BASE + 3 + 3 * k, w3c[:, :, bass.ds(n0, 256)], i)
                    load(FF_BASE + 4 + 3 * k, w2r[:, bass.ds(i * 4 + 2 * k, 2), :], i)
            load(FF_BASE + 3 * FF_STEPS - 1,
                 ffn_w2[0].rearrange("(j p) n -> p j n", p=P)[:, 2 * FF_STEPS - 2:2 * FF_STEPS, :])
            load_in(1)
            ew1 = moe_w1[0].rearrange("e (c p) n -> p (e c) n", p=P)
            ew3 = moe_w3[0].rearrange("e (c p) n -> p (e c) n", p=P)
            ew2 = moe_w2[0].rearrange("e (j p) n -> p (e j) n", p=P)

            def load_up(base, e, n0, i):
                for k, w in enumerate((ew1, ew3)):
                    for half in range(2):
                        load(base + 2 * k + half,
                             w[:, bass.ds(e * DC + 4 * half, 4), bass.ds(n0, 512)], i)

            def load_down(base, e, s, i):
                for half in range(2):
                    load(base + half,
                         ew2[:, bass.ds(e * (4 * EX_STEPS) + s * 4 + 2 * half, 2), :], i)

            def expert(b, e):
                it = (b * EXPERTS + e) * EX_STEPS
                load_up(EX_BASE, e, 0, it)
                with sp.Fori(1, EX_STEPS) as s:
                    load_up(EX_BASE + 4, e, s * 512, it + s - 1)
                    load_down(EX_BASE + 8, e, s - 1, it + s - 1)
                load_down(EX_BASE + 4 + 6 * (EX_STEPS - 1), e, EX_STEPS - 1, it)

            with sp.Fori(0, EXPERTS) as e:
                expert(0, e)
            sp.wait_ge(blocks_ready, 1)
            nb = sp.value_load(blocks_i[0:1, 0:1], min_val=1, max_val=3)
            with sp.If(nb > 1):
                with sp.Fori(1, nb) as b:
                    with sp.Fori(0, EXPERTS) as e:
                        expert(b, e)

        @block.gpsimd
        def _(pool):
            steps = [0]

            def link(ins):
                steps[0] += 1
                ins.then_inc(pool_step, 1)
                pool.wait_ge(pool_step, steps[0])

            pool.memset(gate_w[:, :, :, :, :], 0.0).then_inc(pool_step, 1)
            pool.memset(ident[:, :], 0.0).then_inc(pool_step, 1)
            pool.memset(ones[:, :], 1.0).then_inc(pool_step, 1)
            pool.memset(valid, 1.0).then_inc(pool_step, 1)
            pool.memset(eps, EPS).then_inc(pool_step, 1)
            steps[0] = 5
            pool.wait_ge(pool_step, 5)
            link(pool.affine_select(out=ident[:, :], in_=ident[:, :], compare_op=ALU.not_equal,
                                    fill=1.0, base=0, pattern=[[-1, P]], channel_multiplier=1))
            pool.affine_select(out=before[:, :], in_=ones[:, :], compare_op=ALU.is_gt, fill=0.0,
                               base=0, pattern=[[1, P]], channel_multiplier=-1
                               ).then_inc(pool_step, 1)
            pool.affine_select(out=valid, in_=valid, compare_op=ALU.is_gt, fill=0.0, base=T,
                               pattern=[[-P, 3]], channel_multiplier=-1).then_inc(pool_step, 1)
            pool.iota(iota[:, :], pattern=[[1, P]], base=0, channel_multiplier=0,
                      allow_small_or_imprecise_dtypes=True).then_inc(pool_step, 1)
            pool.iota(rank, pattern=[[-1, EXPERTS]], base=EXPERTS, channel_multiplier=0,
                      allow_small_or_imprecise_dtypes=True).then_inc(pool_step, 1)
            pool.iota(xor_st[:, 0, :], pattern=[[0, P]], base=0, channel_multiplier=1
                      ).then_inc(pool_step, 1)
            pool.iota(xor_st[:, 1, :], pattern=[[1, P]], base=0, channel_multiplier=0
                      ).then_inc(pool_step, 1)
            steps[0] += 6
            pool.wait_ge(pool_step, steps[0])
            pool.sem_inc(consts, 1)
            for l in range(DEPTH):
                for k, w in enumerate((w_ra, w_ix)):
                    for half in range(2):
                        rows = slice(64 * half, 64 * half + 64)
                        pool.dma_start(gate_w[rows, l, k, :, rows],
                                       w[l].rearrange("(j two) c d -> two c j d", two=2)[half]
                                       ).then_inc(gw_landed, 16)
            pool.dma_start(rw[:, :, :], router_w[0].rearrange("(c p) e -> p c e", p=P)
                           ).then_inc(rw_landed, 16)
            pool.dma_start(conv_sample[:, :, 0:2, :], state_conv[:, :, 1:3, :]
                           ).then_inc(rows_stored, 16)

            for l in range(DEPTH):
                pool.wait_ge(q_sig, l + 1)
                pool.tensor_tensor(zq[:, :, :], zq[:, :, :], xc[:, :, :], ALU.mult
                                   ).then_inc(q_ready, 1)
                pool.wait_ge(cum_ready, l + 1)
                for k in range(8):
                    half = 1 << k
                    if k >= 3:
                        pool.wait_ge(sc_done, PRODUCTS * l + (2 * (k - 3) + 4))
                    parts = lambda a: a[:, :, 0:NPROMPT].rearrange(
                        "p h (n two m) -> p h n two m", two=2, m=half)
                    cv, xv = parts(cum), parts(lev[k % 3])
                    mid = cv[:, :, :, 0, half - 1:half].broadcast_to(
                        [P, HEADS, NPROMPT // (2 * half), half])
                    pool.tensor_tensor(xv[:, :, :, 0, :], mid, cv[:, :, :, 0, :], ALU.subtract
                                       ).then_inc(lev_in, 1)
                    pool.tensor_tensor(xv[:, :, :, 1, :], cv[:, :, :, 1, :], mid, ALU.subtract
                                       ).then_inc(lev_in, 1)
                pool.wait_ge(sc_done, PRODUCTS * l + 14)
                pool.tensor_tensor(lev[2][:, :, 0:NPROMPT],
                                   cum[:, :, NPROMPT - 1:NPROMPT].broadcast_to(
                                       [P, HEADS, NPROMPT]), cum[:, :, 0:NPROMPT], ALU.subtract
                                   ).then_inc(kd_in, 1)
                pool.wait_ge(z_free, 4 + 24 * l + 20)
                link(pool.tensor_tensor(zf[:, :, :], zr[:, :, :], zr[:, :, :], ALU.mult))
                link(pool.tensor_scalar(zf[:, :, :], zf[:, :, :], 0.044715, 1.0, ALU.mult,
                                        ALU.add))
                pool.tensor_tensor(zf[:, :, :], zf[:, :, :], zr[:, :, :], ALU.mult
                                   ).then_inc(gelu_in, 1)
                pool.wait_ge(gelu_sig, l + 1)
                pool.tensor_tensor(zr[:, :, :], zr[:, :, :], zf[:, :, :], ALU.mult
                                   ).then_inc(gelu_ready, 1)
                pool.wait_ge(st_landed, 16 * (l + 1))
                for b in range(NSAMPLE):
                    pool.wait_ge(st_read, NSAMPLE * l + b + 1)
                    f_b = forget[:, :, NPROMPT + b:NPROMPT + b + 1].broadcast_to([P, HEADS, P])
                    st = hstate[:, HEADS * b:HEADS * (b + 1), :]
                    pool.tensor_tensor(st, st, f_b, ALU.mult).then_inc(st_decayed, 1)
                pool.wait_ge(fin_done, l + 1)
                pool.wait_ge(vs_split, l + 1)
                for b in range(NSAMPLE):
                    if b == 1:
                        pool.wait_ge(om_ready, l + 1)
                    if b >= 2:
                        pool.wait_ge(kv_done, NSAMPLE * l + b - 1)
                    for part in range(2):
                        v_b = vs[:, part, :, b:b + 1].bitcast(F32).broadcast_to([P, HEADS, P])
                        pool.tensor_tensor(v_diag[b % 2][:, part, :, :],
                                           ident[:, None, :].broadcast_to([P, HEADS, P]), v_b,
                                           ALU.mult).then_inc(diag_ready, 1)
                pool.wait_ge(st_new, NSAMPLE * HEADS * (l + 1))
                pool.dma_start(hgrn_sample[l].rearrange("b h k v -> k (b h) v"), hstate[:, :, :]
                               ).then_inc(st_stored, 16)
                pool.wait_ge(fin_ready, l + 1)
                pool.dma_start(hgrn_prompt[l, 0].rearrange("h k v -> k h v"), s_fin[:, :, :]
                               ).then_inc(fin_stored, 16)
                pool.wait_ge(rows_ready, l + 1)
                rows = lambda a, n: outs_t[a:a + n, :]
                pool.dma_start(lru_prompt[l].rearrange("a (j p) -> (a j) p", p=P),
                               rows(O_LRUP, 4)).then_inc(rows_stored, 16)
                pool.dma_start(conv_prompt[l].rearrange("a t (j p) -> (a t j) p", p=P),
                               rows(O_CONVP, 12)).then_inc(rows_stored, 16)
                pool.dma_start(lru_sample[l].rearrange("b (j p) -> (b j) p", p=P),
                               rows(O_LRUS, 32)).then_inc(rows_stored, 16)
                pool.dma_start(conv_sample[l, :, 2, :].rearrange("b (j p) -> b j p", p=P),
                               rows(O_XRS, 32)).then_inc(rows_stored, 16)
            pool.wait_ge(st_stored, 16 * DEPTH)
            pool.wait_ge(fin_stored, 16 * DEPTH)
            pool.wait_ge(rows_stored, 16 * (1 + 4 * DEPTH))

        @block.scalar
        def _(act):
            steps = [0]

            def link(ins):
                steps[0] += 1
                ins.then_inc(act_step, 1)
                act.wait_ge(act_step, steps[0])

            def have_table(func):
                link(act.activation(unused, eps, func))

            def hi(base, i=0):
                r, s, lands, u = unit_of(base, i)
                act.wait_ge(landed[r], lands)
                if not isinstance(u, int) or u >= SPLIT:
                    act.wait_ge(used, u - SPLIT + 1)
                act.activation(w_hi[:, s, :], raw[:, r, :], ACT.Copy).then_inc(hi_made, 1)

            vectors = ((norm1_g, V_N1, 16), (norm2_g, V_N2, 16), (final_norm_g, V_NF, 8),
                       (lower_bounds, V_LB, 8), (hg_norm_g, V_HG, 8), (conv_w, V_CW, 32),
                       (conv_b, V_CB, 8), (b_ra, V_RA, 8), (b_ix, V_IX, 8), (lru_lambda, V_LAM, 8))
            for v, r0, n in vectors:
                flat = {1: "(j p) -> j p", 2: "l (j p) -> (l j) p",
                        3: "l t (j p) -> (l t j) p"}[len(v.shape)]
                act.dma_start(vec_rows[r0:r0 + n, 0, :], v.rearrange(flat, p=P)
                              ).then_inc(vec_landed, 16)
            act.dma_start(vec_rows[0:64, 1, :], state_lru.rearrange("l b (j p) -> (l b j) p", p=P)
                          ).then_inc(vec_landed, 16)
            for l in range(DEPTH):
                act.dma_start(vec_rows[0:96, 2 + l, :],
                              state_conv[l].rearrange("b t (j p) -> (b t j) p", p=P)
                              ).then_inc(vec_landed, 16)
            act.sem_inc(z_free, 4)

            def norm(n, chunk_sum, unit=None):
                have_table(ACT.Sqrt)
                for c in range(DC):
                    act.wait_ge(x_sum, chunk_sum(c))
                    act.activation(sq[:, c, :], xT[:, c, :], ACT.Square).then_inc(sq_ready, 1)
                if unit is not None:
                    hi(unit)
                act.wait_ge(ssq_done, n + 1)
                act.activation(rstd[:, 0, :], ps[:, NORM_BANK[n], 0:T], ACT.Sqrt, bias=eps,
                               scale=1.0 / D).then_inc(root_done, 1)

            def norm_hi(n):
                if n in (1, 3):
                    act.wait_ge(st_stored, 16 * ((n + 1) // 2))
                for c in range(DC):
                    act.wait_ge(h_full, DC * n + c + 1)
                    act.activation(h_hi[:, c, :], hF[:, c, :], ACT.Copy).then_inc(h_hi_made, 1)

            def z_out(l, n):
                act.wait_ge(z_done, 24 * l + n + 1)
                bank, h = ps[:, n % 4, :], n % 4
                group = n // 4
                if group == 3:
                    act.activation(zx[:, h, 3:3 + NPROMPT], bank[:, 0:NPROMPT], ACT.Copy
                                   ).then_inc(act_step, 1)
                    steps[0] += 1
                    cols = outs[:, O_XRS:O_XRS + 32].rearrange("p (b j) -> p j b", j=HEADS)
                    act.activation(cols[:, h, :], bank[:, NPROMPT:T], ACT.Copy
                                   ).then_inc(z_free, 1)
                else:
                    dst = (zf, zq, zv, None, zr, zg)[group]
                    act.activation(dst[:, h, :], bank[:, 0:T], ACT.Copy).then_inc(z_free, 1)

            def mixer(l):
                ib, ob = IN_BASE[l], OUT_BASE[l]
                for u in range(IN_UNITS + SPLIT):
                    if u >= EARLY[l]:
                        hi(ib + u)
                    if l == 0 and u == SPLIT - 1:
                        act.wait_ge(setup_in, 2)
                        act.activation(tmp[:, 8:16], tmp[:, 8:16], ACT.Exp).then_inc(setup_exp, 1)
                        act.activation(tmp[:, 24:32], tmp[:, 24:32], ACT.Exp
                                       ).then_inc(setup_exp, 1)
                    if u == IN_UNITS + SPLIT - 1:
                        act.wait_ge(used, ib + IN_UNITS)
                        act.dma_start(hstate[:, :, :],
                                      state_hgrn[l].rearrange("b h k v -> k (b h) v")
                                      ).then_inc(st_landed, 16)
                    if u >= SPLIT:
                        z_out(l, 2 * (u - SPLIT))
                        z_out(l, 2 * (u - SPLIT) + 1)
                    zs = lambda n: act.wait_ge(z_free, 4 + 24 * l + n)
                    if u == SPLIT + 1:
                        zs(4)
                        act.activation(lev[0][:, :, :], zf[:, :, :], ACT.Sigmoid
                                       ).then_inc(f_sig, 1)
                        act.activation(lev[1][:, :, :], zf[:, :, :], ACT.Sigmoid, scale=-1.0
                                       ).then_inc(f_sig, 1)
                    if u == SPLIT + 3:
                        zs(8)
                        act.activation(xc[:, :, :], zq[:, :, :], ACT.Sigmoid).then_inc(q_sig, 1)
                        act.wait_ge(clamp_ready, l + 1)
                        act.activation(lev[0][:, :, :], lev[0][:, :, :], ACT.Ln
                                       ).then_inc(ln_ready, 1)
                    if u >= LEVEL_LAG:
                        k = u - LEVEL_LAG
                        act.wait_ge(lev_in, 16 * l + 2 * k + 2)
                        x = lev[k % 3][:, :, 0:NPROMPT]
                        act.activation(x, x, ACT.Exp).then_inc(lev_exp, 1)
                act.activation(vs[:, 0, :, :], zv[:, :, NPROMPT:T], ACT.Copy
                               ).then_inc(vs_high, 1)
                act.wait_ge(kd_in, l + 1)
                x = lev[2][:, :, 0:NPROMPT]
                act.activation(x, x, ACT.Exp).then_inc(kd_exp, 1)
                act.wait_ge(z_free, 4 + 24 * (l + 1))
                act.activation(cum[:, :, :], zg[:, :, :], ACT.Sigmoid).then_inc(g_sig, 1)
                act.wait_ge(gelu_in, l + 1)
                act.activation(zf[:, :, :], zf[:, :, :], ACT.Sigmoid, scale=1.5957691216057308
                               ).then_inc(gelu_sig, 1)
                act.wait_ge(v_turned, l + 1)
                act.activation(v_tok[:, :, :, :].rearrange("p c h v -> p (c h v)"),
                               ps[:, 0:2, :].rearrange("p a b -> p (a b)"), ACT.Copy
                               ).then_inc(v_ready, 1)

                def gate(n):
                    act.wait_ge(gates_done, 8 * l + n + 1)
                    j = n % 4
                    bias = vecT[:, (V_RA, V_IX)[n // 4] + 4 * l + j:][:, 0:1]
                    act.activation(lev[1 + n // 4][:, j, :], ps[:, GATE_BANK[n % 3], 0:T],
                                   ACT.Sigmoid, bias=bias).then_inc(gates_ready, 1)

                for n in range(3):
                    gate(n)
                act.wait_ge(kd_turned, l + 1)
                act.activation(k_tok[:, :, :, :].rearrange("p c h v -> p (c h v)"),
                               ps[:, 6:8, :].rearrange("p a b -> p (a b)"), ACT.Copy
                               ).then_inc(kd_tok_ready, 1)
                for n in range(3, 8):
                    gate(n)
                act.wait_ge(gates_ready, 8 * (l + 1))
                for j in range(HEADS):
                    act.activation(zx[:, j, :], lev[1][:, j, :], ACT.Tanh,
                                   scale=crate[:, 4 * l + j:4 * l + j + 1]
                                   ).then_inc(decay_ready, 1)
                act.wait_ge(decay_ready, 8 * l + 4)
                for j in range(HEADS):
                    link(act.activation(lev[1][:, j, :], lev[1][:, j, :], ACT.Exp,
                                        scale=ncrate[:, 4 * l + j:4 * l + j + 1]))
                    act.sem_inc(decay_ready, 1)
                act.wait_ge(fin_done, l + 1)
                if l:
                    act.wait_ge(fin_stored, 16 * l)
                act.activation(s_fin[:, :, :].rearrange("p h v -> p (h v)"), ps[:, 4, :],
                               ACT.Copy).then_inc(fin_ready, 1)
                have_table(ACT.Sqrt)
                act.wait_ge(om_ready, l + 1)
                act.activation(zx[:, :, :], zx[:, :, :], ACT.Sqrt).then_inc(om_root, 1)
                def merge_high(n):
                    c = MERGE_ORDER[n]
                    act.wait_ge(merged, DC * l + n + 1)
                    src = heads[:, c, :] if c < HEADS else xc[:, c - HEADS, :]
                    act.activation(m_hi[:, c, :], src, ACT.Copy).then_inc(m_hi_made, 1)

                have_table(ACT.Ln)
                act.wait_ge(o_ready, l + 1)
                act.wait_ge(gelu_ready, l + 1)
                act.activation(zf[:, :, :], heads[:, :, :], ACT.Square).then_inc(o_sq, 1)
                for n in range(HEADS):
                    merge_high(n)
                act.wait_ge(o_ssq, l + 1)
                link(act.activation(zf[:, :, :], ps[:, 4:8, 0:T], ACT.Ln, bias=eps, scale=1.0 / P))
                act.activation(zf[:, :, :], zf[:, :, :], ACT.Exp, scale=-0.5).then_inc(o_root, 1)
                for n in range(HEADS, DC):
                    merge_high(n)
                hi(ob + 3)
                if l == 0:
                    hi(FF_BASE)
                    hi(FF_BASE + 1)

            act.wait_ge(consts, 1)
            norm(0, lambda c: c + 1, unit=0)
            norm_hi(0)
            mixer(0)
            norm(1, lambda c: 8 + c + 1)
            norm_hi(1)

            def ff_act(s, used_w1):
                act.wait_ge(used, used_w1)
                if not isinstance(s, int):
                    act.wait_ge(ff_g_done, s)
                act.activation(ff_silu[:, :, :], ps[:, 0:2, 0:T], ACT.Silu
                               ).then_inc(ff_silu_done, 1)

            def ff_high(s, parity):
                act.wait_ge(ff_g_done, s + 1)
                act.activation(ff_hi[:, parity, :, :], ff_g[:, :, :], ACT.Copy
                               ).then_inc(ff_hi_done, 1)

            ff_act(0, FF_BASE + 1)
            with act.Fori(0, (FF_STEPS - 1) // 2) as i:
                for k in range(2):
                    s = i * 2 + (k + 1)
                    b = FF_BASE + 2 + 3 * k
                    hi(b, i)
                    ff_high(s - 1, k)
                    hi(b + 1, i)
                    hi(b + 2, i)
                    ff_act(s, i * RAW + (b + 1))
            hi(FF_BASE + 3 * FF_STEPS - 1)
            ff_high(FF_STEPS - 1, 0)
            hi(IN_BASE[1])
            hi(IN_BASE[1] + 1)
            norm(2, lambda c: 16 + 8 * (FF_STEPS - 1) + c + 1)
            norm_hi(2)
            mixer(1)
            norm(3, lambda c: 16 + 8 * FF_STEPS + c + 1)
            for n in range(6):
                t, half = n // 2, n % 2
                rows = TOKEN_TILES[t][2]
                act.wait_ge(ht_turned, n + 1)
                if n == 0:
                    act.wait_ge(ht_zero, 1)
                if n == 4:
                    act.wait_ge(margin_ready, 1)
                    act.activation(rt[:, 9, :, 0], rt[:, 8, :, 0], ACT.Exp
                                   ).then_inc(margin_exp, 1)
                act.activation(h_tok[0:rows, 0, t, 512 * half:512 * half + 512],
                               ps[0:rows, TURN_BANK[n % 4], :], ACT.Copy).then_inc(ht_hi, 1)

            def gather_high(it):
                for half in range(2):
                    act.wait_ge(gathered, it * 4 + (half + 1))
                    act.activation(xg[:, 0, 4 * half:4 * half + 4, :],
                                   ps[:, 5 + half, :].rearrange("p (c n) -> p c n", c=4),
                                   ACT.Copy).then_inc(xg_hi, 1)

            def y_high(it):
                act.wait_ge(y_gated, it * 2 + 2)
                act.wait_ge(spread, START + it * DC)
                act.activation(y_ex[:, 0, :], y_f[:, :], ACT.Copy).then_inc(y_hi, 1)

            gather_high(0)
            act.wait_ge(blocks_ready, 1)
            nb = act.value_load(blocks_i[0:1, 0:1], min_val=1, max_val=3)
            with act.Fori(0, nb) as b:
                with act.Fori(0, EXPERTS) as e:
                    it = b * EXPERTS + e
                    s0 = it * EX_STEPS
                    for j in range(3):
                        hi(EX_BASE + j, s0)
                    y_high(it)
                    hi(EX_BASE + 3, s0)

                    def silu(s, w1_used):
                        act.wait_ge(used, w1_used)
                        act.wait_ge(g_done, START + s)
                        act.activation(ex_silu[:, :], ps[:, 0, :], ACT.Silu
                                       ).then_inc(silu_done, 1)

                    def turned_high(s):
                        act.wait_ge(g_turned, START + s + 1)
                        act.activation(gT[:, 0, :, :].rearrange("p j n -> p (j n)"), ps[:, 2, :],
                                       ACT.Copy).then_inc(gT_hi, 1)

                    silu(s0, s0 * RAW + (EX_BASE + 2))
                    with act.Fori(1, EX_STEPS) as s:
                        i = s0 + (s - 1)
                        for j in range(4):
                            hi(EX_BASE + 4 + j, i)
                        turned_high(i)
                        silu(i + 1, i * RAW + (EX_BASE + 6))
                        hi(EX_BASE + 8, i)
                        hi(EX_BASE + 9, i)
                    hi(EX_BASE + EX_UNITS - 2, s0)
                    hi(EX_BASE + EX_UNITS - 1, s0)
                    gather_high(it + 1)
                    turned_high(s0 + (EX_STEPS - 1))
            norm(4, lambda c: 16 + 8 * FF_STEPS + 8 + c + 1)
            for t, t0, n in TOKEN_TILES:
                act.wait_ge(yt_ready, 2 * t + 2)
                dst = (y_prompt[0, t0:t0 + n, :] if t < 2 else
                       y_sample.rearrange("b s d -> (b s) d"))
                act.dma_start(dst, y_rows[0:n, t, :]).then_inc(stored, 16)
            act.wait_ge(stored, 48)

        @block.vector
        def _(dve):
            steps = [0]

            def link(ins):
                steps[0] += 1
                ins.then_inc(dve_step, 1)
                dve.wait_ge(dve_step, steps[0])

            def lo(base, i=0):
                r, s, _, u = unit_of(base, i)
                dve.wait_ge(hi_made, u + 1)
                dve.tensor_tensor(w_lo[:, s, :], raw[:, r, :], w_hi[:, s, :].bitcast(F32),
                                  ALU.subtract).then_inc(split, 1)

            def bc(ap, n):
                return ap.broadcast_to([P, HEADS, n])

            for c in range(DC):
                dve.wait_ge(x_turned, c + 1)
                dve.tensor_copy(xT[:, c, :], ps[:, c % 4, 0:T]).then_inc(x_sum, 1)
            dve.wait_ge(vec_turned, 1)
            link(dve.tensor_copy(vecT[:, 0:V_ROWS], ps[:, 5, 0:V_ROWS]))
            link(dve.tensor_copy(vecT[:, V_SLRU:V_COLS], ps[:, 5, V_SLRU:V_COLS]))
            dve.sem_inc(vec_ready, 1)

            def norm(n, gain, split_it=True):
                dve.wait_ge(root_done, n + 1)
                link(dve.reciprocal(rstd[:, 1, :], rstd[:, 0, :]))
                for c in range(DC + 2):
                    if c < DC:
                        dve.scalar_tensor_tensor(out=hF[:, c, :], in0=xT[:, c, :],
                                                 scalar=vecT[:, gain + c:gain + c + 1],
                                                 in1=rstd[:, 1, :], op0=ALU.mult, op1=ALU.mult
                                                 ).then_inc(h_full, 1)
                    if c >= 2 and split_it:
                        dve.wait_ge(h_hi_made, DC * n + c - 1)
                        dve.tensor_tensor(h_lo[:, c - 2, :], hF[:, c - 2, :],
                                          h_hi[:, c - 2, :].bitcast(F32), ALU.subtract
                                          ).then_inc(h_split, 1)

            t = lambda k: tmp[:, 8 * k:8 * k + 8]

            def setup():
                a, b = vecT[:, V_LB:V_LB + 4], vecT[:, V_LB + 4:V_LB + 8]
                link(dve.tensor_tensor(t(0)[:, 0:4], a, b, ALU.max))
                link(dve.tensor_tensor(t(1)[:, 0:4], a, t(0)[:, 0:4], ALU.subtract))
                dve.tensor_tensor(t(1)[:, 4:8], b, t(0)[:, 0:4], ALU.subtract
                                  ).then_inc(setup_in, 1)
                lam = vecT[:, V_LAM:V_LAM + 8]
                link(dve.tensor_scalar(t(2), lam, -1.0, None, ALU.mult))
                dve.tensor_tensor(t(3), lam, t(2), ALU.min).then_inc(setup_in, 1)
                dve.wait_ge(setup_exp, 2)
                link(dve.tensor_tensor(t(5)[:, 0:4], t(1)[:, 0:4], t(1)[:, 4:8], ALU.add))
                link(dve.reciprocal(t(5)[:, 0:4], t(5)[:, 0:4]))
                link(dve.memset(lbv[:, 0:4], 0.0))
                link(dve.tensor_tensor(lbv[:, 4:8], t(1)[:, 4:8], t(5)[:, 0:4], ALU.mult))
                link(dve.tensor_scalar(omlb, lbv, -1.0, 1.0, ALU.mult, ALU.add))

            def setup_rates():
                link(dve.tensor_scalar(t(5), t(3), 2.0, None, ALU.add))
                link(dve.reciprocal(t(5), t(5)))
                link(dve.tensor_tensor(t(3), t(3), t(5), ALU.mult))
                link(dve.tensor_tensor(t(5), t(3), t(3), ALU.mult))
                link(dve.memset(t(6), 1.0 / 19))
                for k in range(17, 0, -2):
                    link(dve.tensor_tensor(t(6), t(6), t(5), ALU.mult))
                    link(dve.tensor_scalar(t(6), t(6), 1.0 / k, None, ALU.add))
                link(dve.tensor_tensor(t(6), t(6), t(3), ALU.mult))
                link(dve.tensor_scalar(t(2), t(2), 0.0, None, ALU.max))
                link(dve.scalar_tensor_tensor(out=t(2), in0=t(6), scalar=2.0, in1=t(2),
                                              op0=ALU.mult, op1=ALU.add))
                link(dve.tensor_scalar(crate, t(2), 8.0, None, ALU.mult))
                link(dve.tensor_scalar(ncrate, t(2), -8.0, None, ALU.mult))

            def setup_masks():
                dve.wait_ge(consts, 1)
                link(dve.tensor_tensor(xor_st[:, 2, :], xor_st[:, 0, :], xor_st[:, 1, :],
                                       ALU.bitwise_xor))
                link(dve.tensor_tensor(xor_f[:, 0, :], xor_st[:, 2, :], before[:, :], ALU.mult))
                for k in range(7):
                    link(dve.tensor_scalar(xor_f[:, 1, :], xor_f[:, 0, :], float(1 << k), None,
                                           ALU.is_ge))
                    link(dve.scalar_tensor_tensor(out=masks[:, k, :], in0=xor_f[:, 0, :],
                                                  scalar=float(2 << k), in1=xor_f[:, 1, :],
                                                  op0=ALU.is_lt, op1=ALU.mult))

            def mixer(l):
                ib, ob = IN_BASE[l], OUT_BASE[l]
                v = lambda col: vecT[:, col:col + 1]
                dve.wait_ge(x_sum, 8 if l == 0 else 16 + 8 * FF_STEPS)
                link(dve.memset(zx[:, :, 0:3], 0.0))

                def forget_and_key():
                    dve.wait_ge(f_sig, 2 * l + 2)
                    for h in range(HEADS):
                        k = 4 * l + h
                        link(dve.tensor_scalar(key[:, h, :], lev[1][:, h, :], omlb[:, k:k + 1],
                                               None, ALU.mult))
                        link(dve.tensor_scalar(forget[:, h, :], lev[0][:, h, :],
                                               omlb[:, k:k + 1], lbv[:, k:k + 1],
                                               ALU.mult, ALU.add))
                    dve.sem_inc(f_ready, 1)
                    dve.tensor_scalar(lev[0][:, :, :], forget[:, :, :], TINY, None, ALU.max
                                      ).then_inc(clamp_ready, 1)
                    link(dve.tensor_scalar(lev[1][:, :, :], forget[:, :, :], TINY, None,
                                           ALU.is_lt))
                    link(dve.scalar_tensor_tensor(out=lev[1][:, :, :], in0=zf[:, :, :],
                                                  scalar=-LN_TINY, in1=lev[1][:, :, :],
                                                  op0=ALU.add, op1=ALU.mult))

                def log_forget():
                    dve.wait_ge(ln_ready, l + 1)
                    link(dve.tensor_tensor(lev[0][:, :, :], lev[0][:, :, :], lev[1][:, :, :],
                                           ALU.add))
                    link(dve.memset(lev[1][:, 0, 0:NPROMPT], 1.0))
                    for h in range(HEADS):
                        link(dve.tensor_tensor_scan(cum[:, h, 0:NPROMPT],
                                                    lev[1][:, 0, 0:NPROMPT],
                                                    lev[0][:, h, 0:NPROMPT], 0.0, ALU.mult,
                                                    ALU.add))
                    dve.sem_inc(cum_ready, 1)

                def level_finish(k):
                    if k == 0:
                        dve.wait_ge(q_ready, l + 1)
                    half, x = 1 << k, lev[k % 3]
                    parts = lambda a: a[:, :, 0:NPROMPT].rearrange(
                        "p h (n two m) -> p h n two m", two=2, m=half)
                    xv, qv, kv = parts(x), parts(zq), parts(key)
                    dve.wait_ge(lev_exp, 8 * l + k + 1)
                    dve.tensor_tensor(xv[:, :, :, 0, :], xv[:, :, :, 0, :], kv[:, :, :, 0, :],
                                      ALU.mult).then_inc(lev_ready, 1)
                    dve.tensor_tensor(xv[:, :, :, 1, :], xv[:, :, :, 1, :], qv[:, :, :, 1, :],
                                      ALU.mult).then_inc(lev_ready, 1)

                def take(n, c, k):
                    dve.wait_ge(sc_done, PRODUCTS * l + n + 1)
                    bank = ps[:, 4 + n % 4, :].rearrange("p (h t) -> p h t", h=HEADS)
                    if k is None:
                        ins = dve.tensor_tensor(sc[:, c, :, :], bank, bc(ident[:, None, :], P),
                                                ALU.mult)
                    elif k == 7:
                        ins = dve.tensor_copy(sc[:, c, :, :], bank)
                    else:
                        ins = dve.copy_predicated(sc[:, c, :, :], bc(masks[:, k:k + 1, :], P),
                                                  bank)
                    ins.then_inc(sc_taken, 1)

                def conv(j):
                    if j == 0:
                        dve.wait_ge(z_free, 4 + 24 * l + 16)
                    link(dve.tensor_scalar(xc[:, j, 0:NPROMPT], zx[:, j, 0:NPROMPT],
                                           v(V_CW + 16 * l + j), v(V_CB + 4 * l + j),
                                           ALU.mult, ALU.add))
                    for tap in range(1, TAPS):
                        link(dve.scalar_tensor_tensor(
                            out=xc[:, j, 0:NPROMPT], in0=zx[:, j, tap:tap + NPROMPT],
                            scalar=v(V_CW + 16 * l + 4 * tap + j), in1=xc[:, j, 0:NPROMPT],
                            op0=ALU.mult, op1=ALU.add))

                xs = outs[:, O_XRS:O_XRS + 32].rearrange("p (b j) -> p j b", j=HEADS)
                qk = tmp[:, 32:64].rearrange("p (j b) -> p j b", j=4)
                own = tmp[:, 64:96].rearrange("p (j b) -> p j b", j=4)
                xcs, part = xc[:, :, NPROMPT:T], tmp[:, 0:32].rearrange("p (j b) -> p j b", j=4)

                def conv_samples():
                    old = vecT[:, V_SCONV + 96 * l:V_SCONV + 96 * l + 96].rearrange(
                        "p (b t j) -> p t j b", t=3, j=HEADS)
                    for tap in range(TAPS):
                        w = bc(vecT[:, V_CW + 16 * l + 4 * tap:V_CW + 16 * l + 4 * tap + 4, None],
                               8)
                        src = old[:, tap] if tap < 3 else xs
                        link(dve.tensor_tensor(part if tap else xcs, src, w, ALU.mult))
                        if tap:
                            link(dve.tensor_tensor(xcs, xcs, part, ALU.add))
                    link(dve.tensor_tensor(xcs, xcs,
                                           bc(vecT[:, V_CB + 4 * l:V_CB + 4 * l + 4, None], 8),
                                           ALU.add))
                    cp = outs[:, O_CONVP:O_CONVP + 12].rearrange("p (t j) -> p j t", j=HEADS)
                    link(dve.tensor_copy(cp, zx[:, :, NPROMPT:NPROMPT + 3]))
                    dve.sem_inc(conv_ready, 1)

                def take_level(k):
                    take(2 * k + 2, 0, k)
                    take(2 * k + 3, 1, k)
                    dve.wait_ge(sc_taken, PRODUCTS * l + 2 * k + 4)

                def sample_queries():
                    dve.wait_ge(q_ready, l + 1)
                    qs, ks = zq[:, :, NPROMPT:T], key[:, :, NPROMPT:T]
                    link(dve.tensor_tensor(qk, qs, ks, ALU.mult))
                    dve.tensor_tensor(qs, qs, forget[:, :, NPROMPT:T], ALU.mult
                                      ).then_inc(qf_ready, 1)

                for u in range(IN_UNITS + SPLIT):
                    if u >= EARLY[l]:
                        lo(ib + u)
                    if l == 0 and u == SPLIT - 1:
                        setup()
                    if l == 0 and u == SPLIT:
                        setup_masks()
                    if l == 0 and u == SPLIT + 4:
                        setup_rates()
                    if u == SPLIT + 1:
                        forget_and_key()
                    if u == SPLIT + 3:
                        log_forget()
                    if u >= LEVEL_LAG:
                        k = u - LEVEL_LAG
                        level_finish(k)
                        if k == 1:
                            take(0, 0, None)
                            take(1, 1, None)
                            dve.wait_ge(sc_taken, PRODUCTS * l + 2)
                        if k >= 2:
                            take_level(k - 2)
                    if u == 9:
                        sample_queries()
                    if 10 <= u < 14:
                        conv(u - 10)
                    if u == 13:
                        conv_samples()
                x = lev[2][:, :, 0:NPROMPT]
                dve.wait_ge(vs_high, l + 1)
                dve.tensor_tensor(vs[:, 1, :, :], zv[:, :, NPROMPT:T], vs[:, 0, :, :].bitcast(F32),
                                  ALU.subtract).then_inc(vs_split, 1)
                dve.wait_ge(kd_exp, l + 1)
                dve.tensor_tensor(x, x, key[:, :, 0:NPROMPT], ALU.mult).then_inc(kd_ready, 1)
                take_level(6)
                take(16, 2, 7)
                dve.wait_ge(g_sig, l + 1)
                link(dve.tensor_tensor(zg[:, :, :], zg[:, :, :], cum[:, :, :], ALU.mult))
                dve.wait_ge(gates_ready, 8 * (l + 1))
                link(dve.tensor_tensor(lev[2][:, :, :], lev[2][:, :, :], xc[:, :, :], ALU.mult))
                dve.wait_ge(decay_ready, 8 * (l + 1))
                link(dve.tensor_tensor(cum[:, :, :], lev[1][:, :, :], lev[1][:, :, :], ALU.mult))
                dve.scalar_tensor_tensor(out=zx[:, :, :], in0=cum[:, :, :], scalar=1.0,
                                         in1=zx[:, :, :], op0=ALU.add, op1=ALU.mult
                                         ).then_inc(om_ready, 1)

                def new_state(b):
                    dve.wait_ge(kv_done, NSAMPLE * l + b + 1)
                    dve.wait_ge(st_decayed, NSAMPLE * l + b + 1)
                    for h in range(HEADS):
                        st = hstate[:, HEADS * b + h, :]
                        dve.scalar_tensor_tensor(
                            out=st, in0=ps[:, 5 + b % 3, P * h:P * h + P],
                            scalar=key[:, h, NPROMPT + b:NPROMPT + b + 1], in1=st,
                            op0=ALU.mult, op1=ALU.add).then_inc(st_new, 1)

                dve.wait_ge(om_root, l + 1)
                link(dve.tensor_tensor(lev[2][:, :, :], lev[2][:, :, :], zx[:, :, :], ALU.mult))
                for j in range(HEADS):
                    link(dve.tensor_tensor_scan(xc[:, j, 0:NPROMPT], lev[1][:, j, 0:NPROMPT],
                                                lev[2][:, j, 0:NPROMPT], 0.0, ALU.mult, ALU.add))
                dve.wait_ge(qk_done, l + 1)
                link(dve.tensor_tensor(own, ps[:, 5, 0:HEADS * NSAMPLE].rearrange(
                    "p (j b) -> p j b", j=4), zv[:, :, NPROMPT:T], ALU.mult))
                dve.wait_ge(o_done, l + 1)
                link(dve.tensor_copy(heads[:, :, :], ps[:, 0:4, 0:T]))
                dve.tensor_tensor(heads[:, :, NPROMPT:T], heads[:, :, NPROMPT:T], own, ALU.add
                                  ).then_inc(o_ready, 1)

                h0 = vecT[:, V_SLRU + 32 * l:V_SLRU + 32 * l + 32].rearrange("p (b j) -> p j b",
                                                                            j=HEADS)
                link(dve.tensor_tensor(xcs, h0, lev[1][:, :, NPROMPT:T], ALU.mult))
                link(dve.tensor_tensor(xcs, xcs, lev[2][:, :, NPROMPT:T], ALU.add))
                ls = outs[:, O_LRUS:O_LRUS + 32].rearrange("p (b j) -> p j b", j=HEADS)
                link(dve.tensor_copy(ls, xcs))
                dve.tensor_copy(outs[:, O_LRUP:O_LRUP + 4, None],
                                xc[:, :, NPROMPT - 1:NPROMPT]).then_inc(rows_in, 1)
                dve.wait_ge(rows_in, l + 1)
                dve.wait_ge(gelu_ready, l + 1)
                link(dve.tensor_tensor(xc[:, :, :], xc[:, :, :], zr[:, :, :], ALU.mult))
                dve.sem_inc(merged, HEADS)
                def merge_low(n):
                    c = MERGE_ORDER[n]
                    dve.wait_ge(m_hi_made, DC * l + n + 1)
                    src = heads[:, c, :] if c < HEADS else xc[:, c - HEADS, :]
                    dve.tensor_tensor(m_lo[:, c, :], src, m_hi[:, c, :].bitcast(F32),
                                      ALU.subtract).then_inc(m_split, 1)

                for n in range(HEADS):
                    merge_low(n)
                dve.wait_ge(o_root, l + 1)
                link(dve.tensor_tensor(zf[:, :, :], zf[:, :, :], zg[:, :, :], ALU.mult))
                for h in range(HEADS):
                    dve.scalar_tensor_tensor(out=heads[:, h, :], in0=heads[:, h, :],
                                             scalar=v(V_HG + 4 * l + h), in1=zf[:, h, :],
                                             op0=ALU.mult, op1=ALU.mult).then_inc(merged, 1)
                for n in range(HEADS, DC):
                    merge_low(n)
                for b in range(STATES_FIRST):
                    new_state(b)
                lo(ob + 3)
                dve.wait_ge(rows_turned, l + 1)
                if l:
                    dve.wait_ge(rows_stored, 16 * (1 + 4 * l))
                dve.tensor_copy(outs_t[0:O_COLS, :], ps[0:O_COLS, 4, 0:P]).then_inc(rows_ready, 1)
                for c in range(DC):
                    dve.wait_ge(y_done, (0 if l == 0 else DC + DC * FF_STEPS) + c + 1)
                    dve.tensor_tensor(xT[:, c, :], xT[:, c, :], ps[:, c % 4, 0:T], ALU.add
                                      ).then_inc(x_sum, 1)
                    if STATES_FIRST + c < NSAMPLE:
                        new_state(STATES_FIRST + c)
                    if l == 0 and c in (3, 5):
                        lo(FF_BASE + (c - 3) // 2)

            lo(0)
            norm(0, V_N1)
            mixer(0)
            norm(1, V_N2)

            def ff_gate(s, parity, w3_used):
                dve.wait_ge(used, w3_used)
                dve.wait_ge(ff_silu_done, s + 1)
                dve.wait_ge(ff_split, s)
                dve.tensor_tensor(ff_g[:, :, :], ff_silu[:, :, :], ps[:, 2:4, 0:T], ALU.mult
                                  ).then_inc(ff_g_done, 1)
                dve.wait_ge(ff_hi_done, s + 1)
                dve.tensor_tensor(ff_lo[:, parity, :, :], ff_g[:, :, :],
                                  ff_hi[:, parity, :, :].bitcast(F32), ALU.subtract
                                  ).then_inc(ff_split, 1)

            def ff_add(tiles, chunks=range(DC)):
                for c in chunks:
                    dve.wait_ge(y_done, tiles + (DC + c + 1))
                    dve.wait_ge(x_sum, tiles + (16 + c - 7))
                    dve.tensor_tensor(xT[:, c, :], xT[:, c, :], ps[:, 4 + c % 4, 0:T], ALU.add
                                      ).then_inc(x_sum, 1)

            def ff_step(i, k, add, first=False):
                b = FF_BASE + 2 + 3 * k
                s = i * 2 + (k + 1)
                lo(b, i)
                ff_gate(s - 1, k, i * RAW + (b if first else b - 1))
                if add:
                    ff_add((s - 2) * DC)
                lo(b + 1, i)
                lo(b + 2, i)

            ff_step(0, 0, False, first=True)
            ff_step(0, 1, True)
            with dve.Fori(1, (FF_STEPS - 1) // 2) as i:
                for k in range(2):
                    ff_step(i, k, True)
            lo(FF_BASE + 3 * FF_STEPS - 1)
            ff_gate(FF_STEPS - 1, 0, FF_BASE + 3 * FF_STEPS - 2)
            ff_add((FF_STEPS - 2) * DC)
            lo(IN_BASE[1])
            ff_add((FF_STEPS - 1) * DC, range(0, 4))
            lo(IN_BASE[1] + 1)
            ff_add((FF_STEPS - 1) * DC, range(4, DC))
            norm(2, V_N1 + 8)
            mixer(1)
            norm(3, V_N2 + 8, split_it=False)

            L, E1, W, S1, L2, S2, GATE, CHO, DD, EX, POS, R3 = (rt[:, k, :, :] for k in range(12))
            b3 = lambda a: a[:, :, 0:1].broadcast_to([P, 3, EXPERTS])
            dve.wait_ge(st_stored, 16 * DEPTH)
            dve.wait_ge(fin_stored, 16 * DEPTH)
            dve.wait_ge(rows_stored, 16 * (1 + 4 * DEPTH))
            link(dve.memset(h_tok[:, :, 2, :].bitcast(F32), 0.0))
            dve.sem_inc(ht_zero, 1)
            link(dve.memset(rt[:, :, :, :], 0.0))
            dve.wait_ge(logits_done, 1)
            for t, _, n in TOKEN_TILES:
                link(dve.tensor_copy(L[0:n, t, :], ps[0:n, LOGIT_BANK[t], 0:EXPERTS]))
            rank3 = rank[:, None, :].broadcast_to([P, 3, EXPERTS])

            def turned_tokens_low(n):
                t, half = n // 2, n % 2
                rows = TOKEN_TILES[t][2]
                cols = slice(512 * half, 512 * half + 512)
                dve.wait_ge(ht_hi, n + 1)
                dve.tensor_tensor(h_tok[0:rows, 1, t, cols], ps[0:rows, TURN_BANK[n % 4], :],
                                  h_tok[0:rows, 0, t, cols].bitcast(F32), ALU.subtract
                                  ).then_inc(ht_split, 1)

            def first_best(src, sel, best):
                link(dve.tensor_reduce(best[:, :, 0:1], src, AX.X, ALU.max))
                link(dve.tensor_tensor(E1, src, b3(best), ALU.is_equal))
                link(dve.tensor_tensor(W, E1, rank3, ALU.mult))
                link(dve.tensor_reduce(E1[:, :, 0:1], W, AX.X, ALU.max))
                link(dve.tensor_tensor(sel, W, b3(E1), ALU.is_equal))

            first_best(L, S1, GATE)
            link(dve.scalar_tensor_tensor(out=L2, in0=S1, scalar=-3.0e38, in1=L, op0=ALU.mult,
                                          op1=ALU.add))
            first_best(L2, S2, CHO)
            dve.tensor_tensor(DD[:, :, 0:1], CHO[:, :, 0:1], GATE[:, :, 0:1], ALU.subtract
                              ).then_inc(margin_ready, 1)
            dve.wait_ge(margin_ready, 1)
            link(dve.tensor_tensor(W, S1, S2, ALU.add))
            dve.tensor_tensor(CHO, W, valid[:, :, None].broadcast_to([P, 3, EXPERTS]), ALU.mult
                              ).then_inc(chosen_ready, 1)
            dve.wait_ge(chosen_ready, 1)
            link(dve.tensor_scalar(W, CHO, -8192.0, 8192.0, ALU.mult, ALU.add))
            turned_tokens_low(0)
            turned_tokens_low(1)
            dve.wait_ge(pos_done, 1)
            link(dve.tensor_tensor(place[:, :, 0:EXPERTS], W,
                                   ps[:, 1, 0:24].rearrange("p (t e) -> p t e", t=3), ALU.add))
            link(dve.tensor_scalar(place[:, :, EXPERTS:EXPERTS + 1], place[:, :, 0:1],
                                   -float(SLOTS), None, ALU.add))
            def make_pick(it, column):
                dve.wait_ge(pickT_done, START + it)
                for t in range(3):
                    dve.tensor_scalar(pick[:, t, :], iota[:, :],
                                      place[:, t, bass.ds(column, 1)], None, ALU.is_equal
                                      ).then_inc(pick_ready, 1)

            make_pick(0, 0)
            for n in range(2, 6):
                turned_tokens_low(n)
            link(dve.tensor_reduce(R3[:, 0, 0:1], ps[:, 1, 24:32], AX.X, ALU.max))
            link(dve.tensor_scalar(R3[:, 0, 1:2], R3[:, 0, 0:1], float(SLOTS) + 0.5, 1.0,
                                   ALU.is_gt, ALU.add))
            link(dve.scalar_tensor_tensor(out=blocks_i[:, 0:1], in0=R3[:, 0, 0:1],
                                          scalar=2.0 * SLOTS + 0.5, in1=R3[:, 0, 1:2],
                                          op0=ALU.is_gt, op1=ALU.add))
            dve.sem_inc(blocks_ready, 1)
            dve.wait_ge(margin_exp, 1)
            link(dve.tensor_scalar(DD[:, :, 1:2], EX[:, :, 0:1], 1.0, None, ALU.add))
            link(dve.reciprocal(DD[:, :, 2:3], DD[:, :, 1:2]))
            link(dve.tensor_tensor(DD[:, :, 3:4], DD[:, :, 2:3], EX[:, :, 0:1], ALU.mult))
            link(dve.tensor_tensor(W, S1, DD[:, :, 2:3].broadcast_to([P, 3, EXPERTS]), ALU.mult))
            link(dve.tensor_tensor(E1, S2, DD[:, :, 3:4].broadcast_to([P, 3, EXPERTS]), ALU.mult))
            dve.tensor_tensor(GATE, W, E1, ALU.add).then_inc(gates_known, 1)
            dve.wait_ge(ht_split, 6)
            link(dve.memset(ps[:, 3:5, :], 0.0))
            link(dve.memset(gslot, 0.0))
            link(dve.memset(pickT[:, :].bitcast(F32), 0.0))
            for count in (added, y_split, g_done, gT_split, pickT_ready):
                dve.sem_inc(count, START)

            def gather_low(it):
                for half in range(2):
                    dve.wait_ge(gathered, it * 4 + (3 + half))
                    dve.tensor_copy(xg[:, 1, 4 * half:4 * half + 4, :],
                                    ps[:, 5 + half, :].rearrange("p (c n) -> p c n", c=4)
                                    ).then_inc(xg_lo, 1)

            def y_gate(it):
                dve.wait_ge(used, it * EX_UNITS + EX_BASE)
                dve.wait_ge(pickT_ready, START + it * 2)
                dve.wait_ge(y_split, START + it)
                for half in range(2):
                    dve.tensor_scalar(y_f[:, 512 * half:512 * half + 512], ps[:, 3 + half, :],
                                      gslot, None, ALU.mult).then_inc(y_gated, 1)

            def y_low(it):
                dve.wait_ge(y_hi, it + 1)
                dve.tensor_tensor(y_ex[:, 1, :], y_f[:, :], y_ex[:, 0, :].bitcast(F32),
                                  ALU.subtract).then_inc(y_split, 1)

            def add(it, c):
                dve.wait_ge(spread, START + it * DC + (c + 1))
                dve.wait_ge(added, START + it * DC + c)
                dve.tensor_tensor(xT[:, c, :], xT[:, c, :], ps[:, 5 + c % 2, 0:T],
                                  ALU.add).then_inc(added, 1)

            gather_low(0)
            nb = dve.value_load(blocks_i[0:1, 0:1], min_val=1, max_val=3)
            with dve.Fori(0, nb) as b:
                with dve.Fori(0, EXPERTS) as e:
                    it = b * EXPERTS + e
                    s0 = it * EX_STEPS
                    lo(EX_BASE, s0)
                    lo(EX_BASE + 1, s0)
                    y_gate(it)
                    lo(EX_BASE + 2, s0)
                    y_low(it)
                    lo(EX_BASE + 3, s0)

                    def gate(s, w3_used):
                        dve.wait_ge(used, w3_used)
                        dve.wait_ge(silu_done, s + 1)
                        dve.wait_ge(g_turned, START + s)
                        dve.tensor_tensor(ex_g[:, :], ex_silu[:, :], ps[:, 1, :], ALU.mult
                                          ).then_inc(g_done, 1)

                    def turned_low(s):
                        dve.wait_ge(gT_hi, s + 1)
                        dve.tensor_tensor(gT[:, 1, :, :].rearrange("p j n -> p (j n)"),
                                          ps[:, 2, :],
                                          gT[:, 0, :, :].rearrange("p j n -> p (j n)").bitcast(
                                              F32), ALU.subtract).then_inc(gT_split, 1)

                    def step(i, w3_used, spreading=False):
                        lo(EX_BASE + 4, i)
                        gate(i, i * RAW + w3_used)
                        for j in range(1, 4):
                            lo(EX_BASE + 4 + j, i)
                            if spreading:
                                add(it, 2 * j - 2)
                                add(it, 2 * j - 1)
                        turned_low(i)
                        lo(EX_BASE + 8, i)
                        if spreading:
                            add(it, DC - 2)
                            add(it, DC - 1)
                            dve.wait_ge(pickT_done, START + it + 1)
                            dve.tensor_copy(pickT[:, :], ps[:, 7, 0:T]).then_inc(pickT_ready, 1)
                            dve.tensor_copy(gslot, ps[:, 7, T:T + 1]).then_inc(pickT_ready, 1)
                        lo(EX_BASE + 9, i)

                    step(s0, EX_BASE + 4, spreading=True)
                    make_pick(it + 1, e + 1)
                    with dve.Fori(2, EX_STEPS) as s:
                        step(s0 + (s - 1), EX_BASE + 2)
                    lo(EX_BASE + EX_UNITS - 2, s0)
                    lo(EX_BASE + EX_UNITS - 1, s0)
                    gate(s0 + (EX_STEPS - 1), s0 * RAW + (EX_BASE + EX_UNITS - 4))
                    turned_low(s0 + (EX_STEPS - 1))
                    gather_low(it + 1)
                dve.wait_ge(pick_ready, (b * EXPERTS + EXPERTS) * 3 + 3)
                dve.tensor_scalar(place[:, :, :], place[:, :, :], -float(SLOTS), None, ALU.add
                                  ).then_inc(pos_moved, 1)
                dve.wait_ge(pos_moved, b + 1)
            y_gate(nb * EXPERTS)
            for c in range(DC):
                add(nb * EXPERTS, c)
                dve.wait_ge(added, START + nb * (EXPERTS * DC) + (c + 1))
                dve.sem_inc(x_sum, 1)
            norm(4, V_NF, split_it=False)
            for n in range(6):
                t, half = n // 2, n % 2
                rows = TOKEN_TILES[t][2]
                dve.wait_ge(yt_turned, n + 1)
                dve.tensor_copy(y_rows[0:rows, t, 512 * half:512 * half + 512],
                                ps[0:rows, half, :]).then_inc(yt_ready, 1)

        @block.tensor
        def _(pe):
            def mm3(out, l_hi, l_lo, r_hi, r_lo, start, stop):
                pe.matmul(out, l_hi, r_hi, start=start, stop=False)
                pe.matmul(out, l_hi, r_lo, start=False, stop=False)
                return pe.matmul(out, l_lo, r_hi, start=False, stop=stop)

            pe.wait_ge(consts, 1)
            pe.wait_ge(x_landed, 32)
            for c in range(DC):
                if c >= 4:
                    pe.wait_ge(x_sum, c - 3)
                for t, t0, n in TOKEN_TILES:
                    ins = pe.transpose(ps[:, c % 4, t0:t0 + n],
                                       x_rows[0:n, t, c * P:(c + 1) * P], ident[0:n, 0:n])
                ins.then_inc(x_turned, 1)
            def norm(n):
                for c in range(DC):
                    pe.wait_ge(sq_ready, DC * n + c + 1)
                    ins = pe.matmul(ps[:, NORM_BANK[n], 0:T], ones[:, :], sq[:, c, :],
                                    start=(c == 0), stop=(c == DC - 1))
                ins.then_inc(ssq_done, 1)

            def project(base, j, bank, x_hi=h_hi, x_lo=h_lo, order=range(DC), parts=None):
                _, s, _, _ = unit_of(base)
                wh = w_hi[:, s, :].rearrange("p (c n) -> p c n", c=DC)
                wl = w_lo[:, s, :].rearrange("p (c n) -> p c n", c=DC)
                cols = slice(P * j, P * j + P)
                for n, c in enumerate(order):
                    if parts:
                        pe.wait_ge(parts[0], parts[1] + n + 1)
                    ins = mm3(ps[:, bank, 0:T], wh[:, c, cols], wl[:, c, cols], x_hi[:, c, :],
                              x_lo[:, c, :], n == 0, n == DC - 1)
                return ins

            def mixer(l, norm_n):
                ib, ob = IN_BASE[l], OUT_BASE[l]
                n = 0

                def scores(left, right, c, across=False):
                    nonlocal n
                    if n >= 4:
                        pe.wait_ge(sc_taken, PRODUCTS * l + n - 3)
                    for h in range(HEADS):
                        rc = 1 if across else c
                        ins = pe.matmul(ps[:, 4 + n % 4, P * h:P * h + P],
                                        left[:, h, P * c:P * c + P],
                                        right[:, h, P * rc:P * rc + P], start=True, stop=True)
                    ins.then_inc(sc_done, 1)
                    n += 1

                def level(k):
                    pe.wait_ge(lev_ready, 16 * l + 2 * k + 2)
                    scores(lev[k % 3], lev[k % 3], 0, across=(k == 7))
                    if k < 7:
                        scores(lev[k % 3], lev[k % 3], 1)

                for u in range(IN_UNITS):
                    pe.wait_ge(split, ib + u + 1)
                    for j in range(2):
                        t = 2 * u + j
                        pe.wait_ge(z_free, 24 * l + t + 1)
                        project(ib + u, j, t % 4,
                                parts=(h_split, DC * norm_n) if t == 0 else None
                                ).then_inc(z_done, 1)
                    pe.wait_ge(z_done, 24 * l + t + 1)
                    pe.sem_inc(used, 1)
                    if u == 5:
                        pe.wait_ge(q_ready, l + 1)
                        scores(key, zq, 0)
                        scores(key, zq, 1)
                    if u >= 6:
                        level(u - 6)
                pe.wait_ge(z_free, 4 + 24 * l + 24)
                for c in range(2):
                    for h in range(HEADS):
                        ins = pe.transpose(ps[:, c, P * h:P * h + P],
                                           zv[:, h, P * c:P * c + P], ident[:, :])
                ins.then_inc(v_turned, 1)
                level(6)
                level(7)
                pe.wait_ge(conv_ready, l + 1)
                pe.wait_ge(sc_taken, PRODUCTS * l + 14)
                pe.wait_ge(gw_landed, 16 * 8)
                for n8 in range(8):
                    j = n8 % 4
                    if n8 >= 3:
                        pe.wait_ge(gates_ready, 8 * l + n8 - 2)
                    pe.matmul(ps[:, GATE_BANK[n8 % 3], 0:T], gate_w[:, l, n8 // 4, j, :],
                              xc[:, j, :], start=True, stop=True).then_inc(gates_done, 1)
                    if n8 == 2:
                        pe.wait_ge(kd_ready, l + 1)
                        pe.wait_ge(sc_taken, PRODUCTS * l + 16)
                        for c in range(2):
                            for h in range(HEADS):
                                ins = pe.transpose(ps[:, 6 + c, P * h:P * h + P],
                                                   lev[2][:, h, P * c:P * c + P], ident[:, :])
                        ins.then_inc(kd_turned, 1)
                pe.wait_ge(v_ready, l + 1)
                pe.wait_ge(kd_tok_ready, l + 1)
                pe.wait_ge(sc_taken, PRODUCTS * (l + 1))
                for h in range(HEADS):
                    for c in range(2):
                        ins = pe.matmul(ps[:, 4, P * h:P * h + P], k_tok[:, c, h, :],
                                        v_tok[:, c, h, :], start=(c == 0), stop=(c == 1))
                ins.then_inc(fin_done, 1)
                pe.wait_ge(gates_ready, 8 * (l + 1))
                for h in range(HEADS):
                    pe.matmul(ps[:, h, 0:P], v_tok[:, 0, h, :], sc[:, 0, h, :], start=True,
                              stop=True)
                    pe.matmul(ps[:, h, P:2 * P], v_tok[:, 0, h, :], sc[:, 2, h, :], start=True,
                              stop=False)
                    pe.matmul(ps[:, h, P:2 * P], v_tok[:, 1, h, :], sc[:, 1, h, :], start=False,
                              stop=True)
                pe.wait_ge(qf_ready, l + 1)
                pe.matmul(ps[:, 5, 0:HEADS * NSAMPLE], ones[:, :], tmp[:, 32:64], start=True,
                          stop=True).then_inc(qk_done, 1)
                pe.wait_ge(st_landed, 16 * (l + 1))
                for b in range(NSAMPLE):
                    for h in range(HEADS):
                        col = NPROMPT + b
                        ins = pe.matmul(ps[:, h, col:col + 1], hstate[:, HEADS * b + h, :],
                                        zq[:, h, col:col + 1], start=True, stop=True)
                    ins.then_inc(st_read, 1)
                pe.wait_ge(st_read, NSAMPLE * (l + 1))
                pe.sem_inc(o_done, 1)

                def spread_value(b):
                    pe.wait_ge(diag_ready, 2 * (NSAMPLE * l + b + 1))
                    if b < 3:
                        pe.wait_ge(o_root, l + 1)
                    else:
                        pe.wait_ge(st_new, HEADS * (NSAMPLE * l + b - 2))
                    for part in range(2):
                        ins = pe.matmul(ps[:, 5 + b % 3, :], ones_r[:, :],
                                        v_diag[b % 2][:, part, :, :].rearrange("p h v -> p (h v)"),
                                        start=(part == 0), stop=(part == 1))
                    ins.then_inc(kv_done, 1)

                pe.wait_ge(o_sq, l + 1)
                pe.wait_ge(fin_ready, l + 1)
                for h in range(HEADS):
                    ins = pe.matmul(ps[:, 4 + h, 0:T], ones[:, :], zf[:, h, :], start=True,
                                    stop=True)
                ins.then_inc(o_ssq, 1)
                pe.wait_ge(o_root, l + 1)
                pe.wait_ge(rows_in, l + 1)
                pe.transpose(ps[0:O_COLS, 4, 0:P], outs[:, :], ident[:, :]
                             ).then_inc(rows_turned, 1)
                for b in range(STATES_FIRST):
                    spread_value(b)
                n0 = 0 if l == 0 else DC + DC * FF_STEPS
                xs = 8 if l == 0 else 16 + 8 * FF_STEPS
                for u in range(OUT_UNITS):
                    pe.wait_ge(split, ob + u + 1)
                    for j in range(2):
                        c = 2 * u + j
                        if c >= 4:
                            pe.wait_ge(x_sum, xs + c - 3)
                        project(ob + u, j, c % 4, m_hi, m_lo, MERGE_ORDER,
                                (m_split, DC * l) if c == 0 else None).then_inc(y_done, 1)
                        if STATES_FIRST + c < NSAMPLE:
                            spread_value(STATES_FIRST + c)
                    pe.wait_ge(y_done, n0 + c + 1)
                    pe.sem_inc(used, 1)

            norm(0)
            pe.wait_ge(vec_landed, 16 * 13)
            for k, (col, n) in enumerate(((0, V_ROWS), (V_SLRU, 64), (V_SCONV, 96),
                                          (V_SCONV + 96, 96))):
                ins = pe.transpose(ps[:, 5, col:col + n], vec_rows[0:n, k, :], ident[0:n, 0:n])
            ins.then_inc(vec_turned, 1)
            mixer(0, 0)
            norm(1)
            def up(base, i, bank, parts=None):
                pe.wait_ge(split, i * RAW + (base + 1))
                for j in range(2):
                    ins = project(base, j, bank + j, parts=parts if j == 0 else None)
                ins.then_inc(used, 1)

            def down(base, i, parity, s):
                _, sl, _, _ = unit_of(base)
                wh = w_hi[:, sl, :].rearrange("p (j n) -> p j n", j=2)
                wl = w_lo[:, sl, :].rearrange("p (j n) -> p j n", j=2)
                pe.wait_ge(split, i * RAW + (base + 1))
                pe.wait_ge(ff_split, s + 1)
                for c in range(DC):
                    pe.wait_ge(x_sum, s * DC + (16 + c - 3))
                    for j in range(2):
                        ins = mm3(ps[:, 4 + c % 4, 0:T], wh[:, j, c * P:(c + 1) * P],
                                  wl[:, j, c * P:(c + 1) * P], ff_hi[:, parity, j, :],
                                  ff_lo[:, parity, j, :], j == 0, j == 1)
                    ins.then_inc(y_done, 1)
                pe.wait_ge(y_done, s * DC + 2 * DC)
                pe.sem_inc(used, 1)

            up(FF_BASE, 0, 0, parts=(h_split, DC))
            up(FF_BASE + 1, 0, 2)
            with pe.Fori(0, (FF_STEPS - 1) // 2) as i:
                for k in range(2):
                    s = i * 2 + (k + 1)
                    b = FF_BASE + 2 + 3 * k
                    pe.wait_ge(ff_silu_done, s)
                    up(b, i, 0)
                    pe.wait_ge(ff_g_done, s)
                    up(b + 1, i, 2)
                    down(b + 2, i, k, s - 1)
            down(FF_BASE + 3 * FF_STEPS - 1, 0, 0, FF_STEPS - 1)
            norm(2)
            mixer(1, 2)
            norm(3)

            pe.wait_ge(rw_landed, 16)
            for c in range(DC):
                pe.wait_ge(h_full, 3 * DC + c + 1)
                for t, t0, n in TOKEN_TILES:
                    ins = pe.matmul(ps[0:n, LOGIT_BANK[t], 0:EXPERTS], hF[:, c, t0:t0 + n],
                                    rw[:, c, :], start=(c == 0), stop=(c == DC - 1))
            ins.then_inc(logits_done, 1)

            def turn_tokens(n):
                t, half = n // 2, n % 2
                _, t0, rows = TOKEN_TILES[t]
                if n >= 4:
                    pe.wait_ge(ht_split, n - 3)
                for c in range(4):
                    ins = pe.transpose(ps[0:rows, TURN_BANK[n % 4], P * c:P * c + P],
                                       hF[:, 4 * half + c, t0:t0 + rows], ident[:, :])
                ins.then_inc(ht_turned, 1)

            for n in range(4):
                turn_tokens(n)
            pe.wait_ge(chosen_ready, 1)
            cho = rt[:, 7, :, :]
            for t in range(3):
                for t2 in range(t + 1):
                    pe.matmul(ps[:, 1, 8 * t:8 * t + 8], (before if t2 == t else ones)[:, :],
                              cho[:, t2, :], start=(t2 == 0), stop=(t2 == t))
            for t in range(3):
                ins = pe.matmul(ps[:, 1, 24:32], ones[:, :], cho[:, t, :], start=(t == 0),
                                stop=(t == 2))
            ins.then_inc(pos_done, 1)
            turn_tokens(4)
            turn_tokens(5)
            for count in (spread, g_turned, pickT_done):
                pe.sem_inc(count, START)

            def gather(it, part):
                pe.wait_ge(pick_ready, it * 3 + 3)
                for half in range(2):
                    if part:
                        pe.wait_ge(xg_hi, it * 2 + (half + 1))
                    for c in range(4):
                        for t in range(3):
                            ins = pe.matmul(ps[:, 5 + half, P * c:P * c + P],
                                            h_tok[:, part, t, (4 * half + c) * P:
                                                  (4 * half + c + 1) * P],
                                            pick[:, t, :], start=(t == 0), stop=(t == 2))
                    ins.then_inc(gathered, 1)

            def scatter(it, c):
                if c == 0:
                    pe.wait_ge(pickT_ready, START + it * 2)
                    pe.wait_ge(y_split, START + it + 1)
                    pe.wait_ge(xg_lo, it * 2 + 2)
                if c >= 2:
                    pe.wait_ge(added, START + it * DC + (c - 1))
                pe.matmul(ps[:, 5 + c % 2, 0:T], y_ex[:, 0, c * P:(c + 1) * P],
                          pickT[:, :], start=True, stop=False)
                pe.matmul(ps[:, 5 + c % 2, 0:T], y_ex[:, 1, c * P:(c + 1) * P],
                          pickT[:, :], start=False, stop=True).then_inc(spread, 1)

            pe.wait_ge(ht_hi, 6)
            gather(0, 0)
            pe.wait_ge(ht_split, 6)
            gather(0, 1)
            pe.wait_ge(gates_known, 1)
            pe.wait_ge(blocks_ready, 1)
            nb = pe.value_load(blocks_i[0:1, 0:1], min_val=1, max_val=3)
            with pe.Fori(0, nb) as b:
                with pe.Fori(0, EXPERTS) as e:
                    it = b * EXPERTS + e
                    s0 = it * EX_STEPS

                    def up_half(base, i, bank, half):
                        _, sl, _, _ = unit_of(base)
                        wh = w_hi[:, sl, :].rearrange("p (c n) -> p c n", c=4)
                        wl = w_lo[:, sl, :].rearrange("p (c n) -> p c n", c=4)
                        pe.wait_ge(split, i * RAW + (base + 1))
                        for c in range(4):
                            k = 4 * half + c
                            ins = mm3(ps[:, bank, :], xg[:, 0, k, :], xg[:, 1, k, :],
                                      wh[:, c, :], wl[:, c, :], k == 0, k == DC - 1)
                        ins.then_inc(used, 1)

                    def turn(s):
                        pe.wait_ge(g_done, START + s + 1)
                        pe.wait_ge(gT_split, START + s)
                        for j in range(4):
                            ins = pe.transpose(ps[:, 2, P * j:P * j + P],
                                               ex_g[:, P * j:P * j + P], ident[:, :])
                        ins.then_inc(g_turned, 1)

                    def down_half(base, i, s, half, first, last):
                        _, sl, _, _ = unit_of(base)
                        wh = w_hi[:, sl, :].rearrange("p (j n) -> p j n", j=2)
                        wl = w_lo[:, sl, :].rearrange("p (j n) -> p j n", j=2)
                        pe.wait_ge(split, i * RAW + (base + 1))
                        if half == 0:
                            pe.wait_ge(gT_split, START + s + 1)
                        for j in range(2):
                            k = 2 * half + j
                            for n in range(2):
                                ins = mm3(ps[:, 3 + n, :], gT[:, 0, k, :], gT[:, 1, k, :],
                                          wh[:, j, 512 * n:512 * n + 512],
                                          wl[:, j, 512 * n:512 * n + 512],
                                          first and k == 0, last and k == 3)
                        ins.then_inc(used, 1)

                    def step(i, s, first):
                        b0 = EX_BASE + 4
                        pe.wait_ge(silu_done, s + 1)
                        up_half(b0, i, 0, 0)
                        if first:
                            scatter(it, 0)
                            scatter(it, 1)
                        up_half(b0 + 1, i, 0, 1)
                        turn(s)
                        if first:
                            scatter(it, 2)
                            scatter(it, 3)
                        up_half(b0 + 2, i, 1, 0)
                        if first:
                            scatter(it, 4)
                            scatter(it, 5)
                        up_half(b0 + 3, i, 1, 1)
                        if first:
                            scatter(it, 6)
                            scatter(it, 7)
                            for t, t0, n in TOKEN_TILES:
                                pe.transpose(ps[:, 7, t0:t0 + n], pick[0:n, t, :].bitcast(F32),
                                             ident[0:n, 0:n])
                            for t in range(3):
                                ins = pe.matmul(ps[:, 7, T:T + 1], pick[:, t, :].bitcast(F32),
                                                rt[:, 6, t, bass.ds(e, 1)], start=(t == 0),
                                                stop=(t == 2))
                            ins.then_inc(pickT_done, 1)
                        down_half(b0 + 4, i, s, 0, first, False)
                        down_half(b0 + 5, i, s, 1, False, False)

                    pe.wait_ge(xg_hi, it * 2 + 2)
                    pe.wait_ge(xg_lo, it * 2 + 2)
                    up_half(EX_BASE, s0, 0, 0)
                    up_half(EX_BASE + 1, s0, 0, 1)
                    up_half(EX_BASE + 2, s0, 1, 0)
                    up_half(EX_BASE + 3, s0, 1, 1)
                    pe.wait_ge(y_gated, it * 2 + 2)
                    step(s0, s0, True)
                    with pe.Fori(2, EX_STEPS) as s:
                        step(s0 + (s - 1), s0 + (s - 1), False)
                    pe.wait_ge(added, START + it * DC + DC)
                    gather(it + 1, 0)
                    turn(s0 + (EX_STEPS - 1))
                    gather(it + 1, 1)
                    down_half(EX_BASE + EX_UNITS - 2, s0, s0 + (EX_STEPS - 1), 0, False, False)
                    down_half(EX_BASE + EX_UNITS - 1, s0, s0 + (EX_STEPS - 1), 1, False, True)
            pe.wait_ge(pickT_ready, START + nb * (EXPERTS * 2))
            pe.wait_ge(xg_lo, nb * (EXPERTS * 2) + 2)
            for c in range(DC):
                pe.wait_ge(y_gated, nb * (EXPERTS * 2) + (1 + c // 4))
                if c >= 2:
                    pe.wait_ge(added, START + nb * (EXPERTS * DC) + (c - 1))
                pe.matmul(ps[:, 5 + c % 2, 0:T], y_f[:, c * P:(c + 1) * P],
                          pickT[:, :].bitcast(F32), start=True, stop=True).then_inc(spread, 1)
            norm(4)
            pe.wait_ge(h_full, 5 * DC)
            for n in range(6):
                t, half = n // 2, n % 2
                _, t0, rows = TOKEN_TILES[t]
                if n >= 2:
                    pe.wait_ge(yt_ready, n - 1)
                for c in range(4):
                    ins = pe.transpose(ps[0:rows, half, P * c:P * c + P],
                                       hF[:, 4 * half + c, t0:t0 + rows], ident[:, :])
                ins.then_inc(yt_turned, 1)


_INS = ['x_prompt', 'x_sample', 'state_hgrn', 'state_lru', 'state_conv', 'norm1_g', 'w_in',
        'lower_bounds', 'hg_norm_g', 'conv_w', 'conv_b', 'w_ra', 'b_ra', 'w_ix', 'b_ix',
        'lru_lambda', 'w_out', 'norm2_g', 'ffn_w1', 'ffn_w3', 'ffn_w2', 'router_w', 'moe_w1',
        'moe_w3', 'moe_w2', 'final_norm_g']
_OUTS = [(1, 256, 1024), (8, 1, 1024), (2, 1, 4, 128, 128), (2, 1, 512), (2, 1, 3, 512),
         (2, 8, 4, 128, 128), (2, 8, 512), (2, 8, 3, 512)]


def kernel(**inputs):
    import numpy as _np
    import concourse.bacc as _bacc
    from concourse import mybir as _mybir
    from concourse.bass_utils import run_bass_kernel_spmd as _run

    nc = _bacc.Bacc("TRN2", target_bir_lowering=False, num_devices=1)
    arrays, args = {}, []
    for name in _INS:
        a = _np.ascontiguousarray(inputs[name])
        arrays[f"in_{name}_dram"] = a
        args.append(nc.dram_tensor(f"in_{name}_dram", a.shape, _mybir.dt.from_np(a.dtype),
                                   kind="ExternalInput").ap())
    for i, shape in enumerate(_OUTS):
        args.append(nc.dram_tensor(f"out_{i}_dram", shape, _mybir.dt.float32,
                                   kind="ExternalOutput").ap())
    trunk(nc, *args)
    r = _run(nc, [arrays], core_ids=[0])
    return tuple(r.results[0][f"out_{i}_dram"] for i in range(len(_OUTS)))
```
